# Optimizing a Trainium2 kernel written in Bass

```python
import functools
import jax, jax.numpy as jnp
from jax import lax
import numpy as np
import math

D_MODEL = 1024
BATCH = 1
SEQ = 512
DEPTH = 1

NSA_HEADS = 8
NSA_KV_GROUPS = 2
NSA_HEAD_DIM = 64
NSA_WIDTH = NSA_HEADS * NSA_HEAD_DIM
NSA_KV_WIDTH = NSA_KV_GROUPS * NSA_HEAD_DIM
CMP_LEN = 32
CMP_STRIDE = 16
CMP_HIDDEN = 256
SEL_BLOCK = 64
SEL_TOPN = 16
WINDOW = 512
Q_BLOCK = 128
ROPE_THETA = 500000.0
ROPE_DIM = NSA_HEAD_DIM // 4

RET_HEADS = 4
RET_QK_DIM = 128
RET_V_DIM = 256
RET_QK_WIDTH = RET_HEADS * RET_QK_DIM
RET_V_WIDTH = RET_HEADS * RET_V_DIM
RET_CHUNK = 128
RET_ROPE_BASE = 10000.0

RMS_EPS = 1e-6
GN_EPS = 1e-6

PROJ_SIZES = (
    NSA_WIDTH,
    NSA_KV_WIDTH,
    NSA_KV_WIDTH,
    NSA_KV_WIDTH,
    NSA_KV_WIDTH,
    NSA_KV_WIDTH,
    NSA_KV_WIDTH,
    NSA_HEADS * 3,
    NSA_WIDTH,
    RET_QK_WIDTH,
    RET_QK_WIDTH,
    RET_V_WIDTH,
    RET_V_WIDTH,
    D_MODEL,
    D_MODEL,
)
PROJ_TOTAL = sum(PROJ_SIZES)


def rms_norm(x, g):
    x32 = x.astype(jnp.float32)
    y = x32 * lax.rsqrt(jnp.mean(x32 * x32, axis=-1, keepdims=True) + RMS_EPS)
    return (y * g.astype(jnp.float32)).astype(x.dtype)

def split_points():
    pts, acc = [], 0
    for s in PROJ_SIZES[:-1]:
        acc += s
        pts.append(acc)
    return pts

def apply_rotary(x, ang):
    half = ang.shape[-1]
    r = 2 * half
    cos = jnp.cos(ang)[:, None, :].astype(x.dtype)
    sin = jnp.sin(ang)[:, None, :].astype(x.dtype)
    x1 = x[..., :half]
    x2 = x[..., half:r]
    return jnp.concatenate([x1 * cos - x2 * sin, x2 * cos + x1 * sin, x[..., r:]], axis=-1)

def masked_softmax(s, mask):
    s = jnp.where(mask, s.astype(jnp.float32), -jnp.inf)
    m = jnp.max(s, axis=-1, keepdims=True)
    m = jnp.where(jnp.isfinite(m), m, 0.0)
    p = jnp.where(mask, jnp.exp(s - m), 0.0)
    return p / jnp.maximum(jnp.sum(p, axis=-1, keepdims=True), jnp.finfo(jnp.float32).tiny)

def compress_blocks(kv, pe, w1, w2):
    S, G, dh = kv.shape
    n_cmp = (S - CMP_LEN) // CMP_STRIDE + 1
    tok_idx = jnp.arange(n_cmp)[:, None] * CMP_STRIDE + jnp.arange(CMP_LEN)[None, :]
    blocks = kv[tok_idx] + pe[None, :, None, :]
    flat = blocks.transpose(0, 2, 1, 3).reshape(n_cmp, G, CMP_LEN * dh)
    return jax.nn.gelu(flat @ w1) @ w2

def nsa_sequence(q, k_cmp_raw, v_cmp_raw, k_sel, v_sel, k_win, v_win, gate,
                 cmp_pe_k, cmp_w1_k, cmp_w2_k, cmp_pe_v, cmp_w1_v, cmp_w2_v):
    S = q.shape[0]
    G, H, dh = NSA_KV_GROUPS, NSA_HEADS, NSA_HEAD_DIM
    hpg = H // G
    scale = dh ** -0.5

    kc = compress_blocks(k_cmp_raw, cmp_pe_k, cmp_w1_k, cmp_w2_k)
    vc = compress_blocks(v_cmp_raw, cmp_pe_v, cmp_w1_v, cmp_w2_v)
    n_cmp = kc.shape[0]
    cmp_start = jnp.arange(n_cmp) * CMP_STRIDE
    cmp_end = cmp_start + CMP_LEN - 1

    n_sel = S // SEL_BLOCK
    n_top = min(SEL_TOPN, n_sel)
    sel_start = jnp.arange(n_sel) * SEL_BLOCK
    overlap = ((cmp_start[:, None] < sel_start[None, :] + SEL_BLOCK)
               & (cmp_start[:, None] + CMP_LEN > sel_start[None, :])).astype(jnp.float32)
    kb = k_sel.reshape(n_sel, SEL_BLOCK, G, dh).transpose(2, 0, 1, 3)
    vb = v_sel.reshape(n_sel, SEL_BLOCK, G, dh).transpose(2, 0, 1, 3)

    k_pad = jnp.pad(k_win, ((WINDOW, 0), (0, 0), (0, 0)))
    v_pad = jnp.pad(v_win, ((WINDOW, 0), (0, 0), (0, 0)))

    n_qb = S // Q_BLOCK
    qb = q.reshape(n_qb, Q_BLOCK, G, hpg, dh)
    gb = gate.reshape(n_qb, Q_BLOCK, G, hpg, 3)
    blk_ids = jnp.arange(n_sel)
    g_idx = jnp.arange(G)[None, :, None]

    def block(args):
        qi, gi, b = args
        t = b * Q_BLOCK + jnp.arange(Q_BLOCK)
        s = jnp.einsum('qghd,cgd->qghc', qi, kc) * scale
        mask_c = (cmp_end[None, :] <= t[:, None])[:, None, None, :]
        p_c = masked_softmax(s, mask_c)
        o_c = jnp.einsum('qghc,cgd->qghd', p_c.astype(vc.dtype), vc)
        imp = jnp.einsum('qgc,cn->qgn', jnp.sum(p_c, axis=2), overlap)
        cur = t // SEL_BLOCK
        valid = blk_ids[None, :] <= cur[:, None]
        forced = ((blk_ids[None, :] == 0) | (blk_ids[None, :] == cur[:, None])
                  | (blk_ids[None, :] == cur[:, None] - 1))
        score = jnp.where(forced[:, None, :], jnp.inf,
                          jnp.where(valid[:, None, :], imp, -jnp.inf))
        _, idx = lax.top_k(score, n_top)
        sel_valid = jnp.take_along_axis(
            jnp.broadcast_to(valid[:, None, :], score.shape), idx, axis=-1)
        ks = kb[g_idx, idx]
        vs = vb[g_idx, idx]
        s = jnp.einsum('qghd,qgnbd->qghnb', qi, ks) * scale
        kpos = idx[..., None] * SEL_BLOCK + jnp.arange(SEL_BLOCK)
        mask_s = sel_valid[..., None] & (kpos <= t[:, None, None, None])
        nk = n_top * SEL_BLOCK
        p_s = masked_softmax(s.reshape(Q_BLOCK, G, hpg, nk),
                             mask_s.reshape(Q_BLOCK, G, 1, nk))
        o_s = jnp.einsum('qghk,qgkd->qghd', p_s.astype(vs.dtype),
                         vs.reshape(Q_BLOCK, G, nk, dh))
        kw = lax.dynamic_slice_in_dim(k_pad, b * Q_BLOCK, Q_BLOCK + WINDOW, axis=0)
        vw = lax.dynamic_slice_in_dim(v_pad, b * Q_BLOCK, Q_BLOCK + WINDOW, axis=0)
        wpos = b * Q_BLOCK - WINDOW + jnp.arange(Q_BLOCK + WINDOW)
        diff = t[:, None] - wpos[None, :]
        mask_w = ((wpos[None, :] >= 0) & (diff >= 0) & (diff < WINDOW))[:, None, None, :]
        s = jnp.einsum('qghd,kgd->qghk', qi, kw) * scale
        p_w = masked_softmax(s, mask_w)
        o_w = jnp.einsum('qghk,kgd->qghd', p_w.astype(vw.dtype), vw)
        g = jax.nn.sigmoid(gi.astype(jnp.float32))
        o = g[..., 0:1] * o_c + g[..., 1:2] * o_s + g[..., 2:3] * o_w
        return o.reshape(Q_BLOCK, H * dh).astype(q.dtype)

    out = lax.map(block, (qb, gb, jnp.arange(n_qb)))
    return out.reshape(S, H * dh)

def retention_sequence(q, k, v):
    S = q.shape[0]
    H, dk, dv, C = RET_HEADS, RET_QK_DIM, RET_V_DIM, RET_CHUNK
    nc = S // C
    log_g = jnp.log(1.0 - 2.0 ** (-5.0 - jnp.arange(H, dtype=jnp.float32)))
    n = jnp.arange(C, dtype=jnp.float32)
    diff = n[:, None] - n[None, :]
    decay_mask = jnp.where(diff >= 0, jnp.exp(jnp.maximum(diff, 0.0)[None] * log_g[:, None, None]), 0.0)
    q_dec = jnp.exp((n[None, :] + 1.0) * log_g[:, None])
    k_dec = jnp.exp((C - 1.0 - n[None, :]) * log_g[:, None])
    chunk_dec = jnp.exp(C * log_g)

    qc = q.reshape(nc, C, H, dk)
    kc = k.reshape(nc, C, H, dk)
    vc = v.reshape(nc, C, H, dv)
    att = jnp.einsum('nihd,njhd->nhij', qc, kc) * decay_mask[None]
    o_inner = jnp.einsum('nhij,njhe->nihe', att, vc)
    kv = jnp.einsum('njhd,hj,njhe->nhde', kc, k_dec, vc).astype(jnp.float32)

    def step(R, kv_i):
        return chunk_dec[:, None, None] * R + kv_i, R

    _, R_prev = lax.scan(step, jnp.zeros((H, dk, dv), jnp.float32), kv)
    o_cross = jnp.einsum('nihd,hi,nhde->nihe', qc, q_dec, R_prev)
    o = (o_inner + o_cross).reshape(S, H, dv).astype(jnp.float32)
    mu = jnp.mean(o, axis=-1, keepdims=True)
    var = jnp.mean(jnp.square(o - mu), axis=-1, keepdims=True)
    o = (o - mu) * lax.rsqrt(var + GN_EPS)
    return o.reshape(S, H * dv).astype(q.dtype)

def first_inputs(seed: int = 0) -> dict:
    key = jax.random.key(seed)
    ks = jax.random.split(key, 16)
    f32 = jnp.float32
    nrm = lambda k, shape, fan_in: jax.random.normal(k, shape, f32) * (fan_in ** -0.5)
    cmp_in = CMP_LEN * NSA_HEAD_DIM
    return {
        "x": jax.random.normal(ks[0], (BATCH, SEQ, D_MODEL), f32),
        "norm_pre": 1.0 + 0.05 * jax.random.normal(ks[1], (D_MODEL,), f32),
        "w_in": nrm(ks[2], (D_MODEL, PROJ_TOTAL), D_MODEL),
        "b_nsa_gate": 0.1 * jax.random.normal(ks[3], (NSA_HEADS * 3,), f32),
        "cmp_pe_k": 0.02 * jax.random.normal(ks[4], (CMP_LEN, NSA_HEAD_DIM), f32),
        "cmp_w1_k": nrm(ks[5], (cmp_in, CMP_HIDDEN), cmp_in),
        "cmp_w2_k": nrm(ks[6], (CMP_HIDDEN, NSA_HEAD_DIM), CMP_HIDDEN),
        "cmp_pe_v": 0.02 * jax.random.normal(ks[7], (CMP_LEN, NSA_HEAD_DIM), f32),
        "cmp_w1_v": nrm(ks[8], (cmp_in, CMP_HIDDEN), cmp_in),
        "cmp_w2_v": nrm(ks[9], (CMP_HIDDEN, NSA_HEAD_DIM), CMP_HIDDEN),
        "w_nsa_o": nrm(ks[10], (NSA_WIDTH, D_MODEL), NSA_WIDTH),
        "w_ret_o": nrm(ks[11], (RET_V_WIDTH, D_MODEL), RET_V_WIDTH),
        "w_out": nrm(ks[12], (D_MODEL, D_MODEL), D_MODEL),
        "norm_post": 1.0 + 0.05 * jax.random.normal(ks[13], (D_MODEL,), f32),
    }

def first_block(x, norm_pre, w_in, b_nsa_gate, cmp_pe_k, cmp_w1_k, cmp_w2_k,
              cmp_pe_v, cmp_w1_v, cmp_w2_v, w_nsa_o, w_ret_o, w_out, norm_post):
    B, S, _ = x.shape
    pos = jnp.arange(S, dtype=jnp.float32)
    nsa_inv = 1.0 / (ROPE_THETA ** (jnp.arange(0, ROPE_DIM, 2, dtype=jnp.float32) / ROPE_DIM))
    nsa_ang = pos[:, None] * nsa_inv[None, :]
    ret_inv = 1.0 / (RET_ROPE_BASE ** jnp.linspace(0.0, 1.0, RET_QK_DIM // 2, dtype=jnp.float32))
    ret_ang = pos[:, None] * ret_inv[None, :]

    for _ in range(DEPTH):
        h = rms_norm(x, norm_pre)
        proj = h @ w_in
        (q_n, k_c, v_c, k_s, v_s, k_w, v_w, g_n, z_n,
         q_r, k_r, v_r, z_r, m_a, m_b) = jnp.split(proj, split_points(), axis=-1)

        kvshape = (B, S, NSA_KV_GROUPS, NSA_HEAD_DIM)
        q_n = apply_rotary(q_n.reshape(B, S, NSA_HEADS, NSA_HEAD_DIM), nsa_ang)
        k_c = apply_rotary(k_c.reshape(kvshape), nsa_ang)
        k_s = apply_rotary(k_s.reshape(kvshape), nsa_ang)
        k_w = apply_rotary(k_w.reshape(kvshape), nsa_ang)
        gate_n = (g_n + b_nsa_gate).reshape(B, S, NSA_HEADS, 3)
        nsa_fn = lambda a, b_, c, d, e, f, g, gt: nsa_sequence(
            a, b_, c, d, e, f, g, gt,
            cmp_pe_k, cmp_w1_k, cmp_w2_k, cmp_pe_v, cmp_w1_v, cmp_w2_v)
        o_a = jax.vmap(nsa_fn)(q_n, k_c, v_c.reshape(kvshape), k_s, v_s.reshape(kvshape),
                               k_w, v_w.reshape(kvshape), gate_n)
        y_a = (o_a * jax.nn.silu(z_n)) @ w_nsa_o

        q_r = apply_rotary(q_r.reshape(B, S, RET_HEADS, RET_QK_DIM), ret_ang)
        k_r = apply_rotary(k_r.reshape(B, S, RET_HEADS, RET_QK_DIM), ret_ang) * (RET_QK_DIM ** -0.5)
        o_b = jax.vmap(retention_sequence)(q_r, k_r, v_r.reshape(B, S, RET_HEADS, RET_V_DIM))
        y_b = (o_b * jax.nn.silu(z_r)) @ w_ret_o

        merged = jax.nn.sigmoid(m_a) * y_a + jax.nn.sigmoid(m_b) * y_b
        x = x + rms_norm(merged @ w_out, norm_post)
    return x


D_MIX = 2 * D_MODEL
ATTN_WIDTH = D_MIX // 2
SB_HEAD_DIM = 64
SB_HEADS = ATTN_WIDTH // SB_HEAD_DIM
SB_BLOCK = 128
SSD_WIDTH = D_MIX - ATTN_WIDTH
SSD_HEAD_DIM = 64
SSD_HEADS = SSD_WIDTH // SSD_HEAD_DIM
SSD_GROUPS = 2
SSD_STATE = 128
SSD_CONV_K = 4
SSD_CHUNK = 128
SSD_CONV_CH = SSD_WIDTH + 2 * SSD_GROUPS * SSD_STATE
IN_SPLITS = (ATTN_WIDTH, ATTN_WIDTH, ATTN_WIDTH, SSD_WIDTH, SSD_WIDTH,
             SSD_GROUPS * SSD_STATE, SSD_GROUPS * SSD_STATE, SSD_HEADS)
D_IN = sum(IN_SPLITS)
MEM_LEN = 256
XA_HEADS = 4
XA_HEAD_DIM = D_MODEL // XA_HEADS
D_FF = 2816
EPS = 1e-6


def rmsnorm(x, g):
    x32 = x.astype(jnp.float32)
    y = x32 * lax.rsqrt(jnp.mean(x32 * x32, axis=-1, keepdims=True) + EPS)
    return (y * g.astype(jnp.float32)).astype(x.dtype)

def swiglu(h, w_gu, w_down):
    gu = h @ w_gu
    g, u = jnp.split(gu, 2, axis=-1)
    return (jax.nn.silu(g) * u) @ w_down

def stick_breaking_attention(q, k, v):
    b_, h_, s_, d_ = q.shape
    scale = 1.0 / math.sqrt(d_)
    outs = []
    for i in range(s_ // SB_BLOCK):
        t0, t1 = i * SB_BLOCK, (i + 1) * SB_BLOCK
        qb = q[:, :, t0:t1].astype(jnp.float32)
        kb = k[:, :, :t1].astype(jnp.float32)
        vb = v[:, :, :t1]
        z = jnp.einsum('bhtd,bhsd->bhts', qb, kb) * scale
        t_idx = t0 + jnp.arange(SB_BLOCK)
        s_idx = jnp.arange(t1)
        causal = s_idx[None, :] < t_idx[:, None]
        log_1mb = jnp.where(causal, jax.nn.log_sigmoid(-z), 0.0)
        suffix = lax.cumsum(log_1mb, axis=3, reverse=True) - log_1mb
        log_a = jnp.where(causal, jax.nn.log_sigmoid(z) + suffix, -jnp.inf)
        a = jnp.exp(log_a)
        outs.append(jnp.einsum('bhts,bhsd->bhtd', a, vb.astype(jnp.float32)))
    return jnp.concatenate(outs, axis=2).astype(v.dtype)

def ssd_chunked(xs, dt, a, bmat, cmat):
    b_, s_, h_, p_ = xs.shape
    L, G, N = SSD_CHUNK, SSD_GROUPS, SSD_STATE
    R = h_ // G
    nc = s_ // L
    x = (xs.astype(jnp.float32) * dt[..., None]).reshape(b_, nc, L, G, R, p_)
    adt = (dt * a).reshape(b_, nc, L, G, R).transpose(0, 3, 4, 1, 2)
    a_cs = jnp.cumsum(adt, axis=-1)
    bc = bmat.astype(jnp.float32).reshape(b_, nc, L, G, N)
    cc = cmat.astype(jnp.float32).reshape(b_, nc, L, G, N)
    tri = jnp.tril(jnp.ones((L, L), dtype=bool))
    diff = a_cs[..., :, None] - a_cs[..., None, :]
    lmat = jnp.exp(jnp.where(tri, diff, -jnp.inf))
    cb = jnp.einsum('bclgn,bcsgn->bcgls', cc, bc)
    y_diag = jnp.einsum('bcgls,bgrcls,bcsgrp->bclgrp', cb, lmat, x)
    decay_states = jnp.exp(a_cs[..., -1:] - a_cs)
    states = jnp.einsum('bclgn,bgrcl,bclgrp->bcgrpn', bc, decay_states, x)
    chunk_decay = jnp.exp(a_cs[..., -1])

    def step(h, inp):
        st, dec = inp
        return h * dec[..., None, None] + st, h

    h0 = jnp.zeros_like(states[:, 0])
    _, states_in = lax.scan(step, h0, (jnp.moveaxis(states, 1, 0),
                                       jnp.moveaxis(chunk_decay, -1, 0)))
    states_in = jnp.moveaxis(states_in, 0, 1)
    y_off = jnp.einsum('bclgn,bcgrpn,bgrcl->bclgrp', cc, states_in, jnp.exp(a_cs))
    return (y_diag + y_off).reshape(b_, s_, h_, p_)

def hybrid_mixer(u, w_in, conv_w, conv_b, dt_bias, a_log, d_skip,
                 ssd_norm_g, attn_norm_g, w_out):
    b_, s_, _ = u.shape
    proj = u @ w_in
    q, k, v, z, xs, bm, cm, dt_raw = jnp.split(proj, np.cumsum(IN_SPLITS)[:-1], axis=-1)
    def heads(t):
        return t.reshape(b_, s_, SB_HEADS, SB_HEAD_DIM).transpose(0, 2, 1, 3)
    o_att = stick_breaking_attention(heads(q), heads(k), heads(v))
    o_att = o_att.transpose(0, 2, 1, 3).reshape(b_, s_, ATTN_WIDTH)
    o_att = rmsnorm(o_att, attn_norm_g)
    xbc = jnp.concatenate([xs, bm, cm], axis=-1)
    xbc = lax.conv_general_dilated(
        xbc, conv_w.astype(xbc.dtype)[:, None, :], window_strides=(1,),
        padding=[(SSD_CONV_K - 1, 0)], dimension_numbers=('NWC', 'WIO', 'NWC'),
        feature_group_count=SSD_CONV_CH)
    xbc = jax.nn.silu(xbc + conv_b)
    xs, bm, cm = jnp.split(xbc, [SSD_WIDTH, SSD_WIDTH + SSD_GROUPS * SSD_STATE], axis=-1)
    xs = xs.reshape(b_, s_, SSD_HEADS, SSD_HEAD_DIM)
    bm = bm.reshape(b_, s_, SSD_GROUPS, SSD_STATE)
    cm = cm.reshape(b_, s_, SSD_GROUPS, SSD_STATE)
    dt = jax.nn.softplus(dt_raw.astype(jnp.float32) + dt_bias.astype(jnp.float32))
    a = -jnp.exp(a_log.astype(jnp.float32))
    y = ssd_chunked(xs, dt, a, bm, cm)
    y = y + d_skip.astype(jnp.float32)[:, None] * xs.astype(jnp.float32)
    y = y.reshape(b_, s_, SSD_WIDTH) * jax.nn.silu(z.astype(jnp.float32))
    y = rmsnorm(y.reshape(b_, s_, SSD_GROUPS, SSD_WIDTH // SSD_GROUPS),
                ssd_norm_g.reshape(SSD_GROUPS, SSD_WIDTH // SSD_GROUPS))
    o_ssd = y.reshape(b_, s_, SSD_WIDTH).astype(u.dtype)
    return jnp.concatenate([o_att, o_ssd], axis=-1) @ w_out

def memory_cross_attention(h, mem_n, wq, wkv, wo):
    b_, s_, _ = h.shape
    q = (h @ wq).reshape(b_, s_, XA_HEADS, XA_HEAD_DIM)
    kv = mem_n @ wkv
    k, v = jnp.split(kv, 2, axis=-1)
    k = k.reshape(b_, MEM_LEN, XA_HEADS, XA_HEAD_DIM)
    v = v.reshape(b_, MEM_LEN, XA_HEADS, XA_HEAD_DIM)
    sc = jnp.einsum('bshd,bmhd->bhsm', q.astype(jnp.float32), k.astype(jnp.float32))
    p = jax.nn.softmax(sc / math.sqrt(XA_HEAD_DIM), axis=-1)
    o = jnp.einsum('bhsm,bmhd->bshd', p, v.astype(jnp.float32)).astype(h.dtype)
    return o.reshape(b_, s_, D_MODEL) @ wo

def second_inputs(seed: int = 0) -> dict:
    key = jax.random.key(seed)
    ks = iter(jax.random.split(key, 40))

    def w(shape, fan_in):
        return jax.random.normal(next(ks), (DEPTH,) + shape, jnp.float32) * fan_in ** -0.5

    def gain(n):
        return 1.0 + 0.02 * jax.random.normal(next(ks), (DEPTH, n), jnp.float32)

    x = jax.random.normal(next(ks), (BATCH, SEQ, D_MODEL), jnp.float32)
    mem = jax.random.normal(next(ks), (BATCH, MEM_LEN, D_MODEL), jnp.float32)
    dt0 = jnp.exp(jax.random.uniform(next(ks), (DEPTH, SSD_HEADS), jnp.float32,
                                     math.log(1e-3), math.log(1e-1)))
    dt_bias = dt0 + jnp.log(-jnp.expm1(-dt0))
    a_log = jnp.log(jax.random.uniform(next(ks), (DEPTH, SSD_HEADS), jnp.float32, 1.0, 16.0))
    return {
        "x": x, "mem": mem,
        "ffn1_pre_g": gain(D_MODEL),
        "ffn1_w_gu": w((D_MODEL, 2 * D_FF), D_MODEL),
        "ffn1_w_down": w((D_FF, D_MODEL), D_FF),
        "ffn1_post_g": gain(D_MODEL),
        "mix_pre_g": gain(D_MODEL),
        "w_in": w((D_MODEL, D_IN), D_MODEL),
        "conv_w": w((SSD_CONV_K, SSD_CONV_CH), SSD_CONV_K),
        "conv_b": 0.02 * jax.random.normal(next(ks), (DEPTH, SSD_CONV_CH), jnp.float32),
        "dt_bias": dt_bias,
        "a_log": a_log,
        "d_skip": 1.0 + 0.1 * jax.random.normal(next(ks), (DEPTH, SSD_HEADS), jnp.float32),
        "ssd_norm_g": gain(SSD_WIDTH),
        "attn_norm_g": gain(ATTN_WIDTH),
        "w_out": w((D_MIX, D_MODEL), D_MIX),
        "mix_post_g": gain(D_MODEL),
        "xa_pre_g": gain(D_MODEL),
        "mem_g": gain(D_MODEL),
        "xa_wq": w((D_MODEL, D_MODEL), D_MODEL),
        "xa_wkv": w((D_MODEL, 2 * D_MODEL), D_MODEL),
        "xa_wo": w((D_MODEL, D_MODEL), D_MODEL),
        "xa_post_g": gain(D_MODEL),
        "ffn2_pre_g": gain(D_MODEL),
        "ffn2_w_gu": w((D_MODEL, 2 * D_FF), D_MODEL),
        "ffn2_w_down": w((D_FF, D_MODEL), D_FF),
        "ffn2_post_g": gain(D_MODEL),
    }

def second_block(x, mem, ffn1_pre_g, ffn1_w_gu, ffn1_w_down, ffn1_post_g,
              mix_pre_g, w_in, conv_w, conv_b, dt_bias, a_log, d_skip,
              ssd_norm_g, attn_norm_g, w_out, mix_post_g,
              xa_pre_g, mem_g, xa_wq, xa_wkv, xa_wo, xa_post_g,
              ffn2_pre_g, ffn2_w_gu, ffn2_w_down, ffn2_post_g):
    h = x
    for l in range(DEPTH):
        f = swiglu(rmsnorm(h, ffn1_pre_g[l]), ffn1_w_gu[l], ffn1_w_down[l])
        h = h + 0.5 * rmsnorm(f, ffn1_post_g[l])
        m = hybrid_mixer(rmsnorm(h, mix_pre_g[l]), w_in[l], conv_w[l], conv_b[l],
                         dt_bias[l], a_log[l], d_skip[l], ssd_norm_g[l],
                         attn_norm_g[l], w_out[l])
        h = h + rmsnorm(m, mix_post_g[l])
        c = memory_cross_attention(rmsnorm(h, xa_pre_g[l]), rmsnorm(mem, mem_g[l]),
                                   xa_wq[l], xa_wkv[l], xa_wo[l])
        h = h + rmsnorm(c, xa_post_g[l])
        f = swiglu(rmsnorm(h, ffn2_pre_g[l]), ffn2_w_gu[l], ffn2_w_down[l])
        h = h + 0.5 * rmsnorm(f, ffn2_post_g[l])
    return h


def setup_inputs(seed=0):
    out = dict(first_inputs(seed))
    for name, value in second_inputs(seed + 1).items():
        if name != "x":
            out[name + "_2"] = value
    return out


def reference(
    x, norm_pre, w_in, b_nsa_gate, cmp_pe_k, cmp_w1_k, cmp_w2_k, cmp_pe_v, cmp_w1_v, cmp_w2_v,
    w_nsa_o, w_ret_o, w_out, norm_post, mem_2, ffn1_pre_g_2, ffn1_w_gu_2, ffn1_w_down_2,
    ffn1_post_g_2, mix_pre_g_2, w_in_2, conv_w_2, conv_b_2, dt_bias_2, a_log_2, d_skip_2,
    ssd_norm_g_2, attn_norm_g_2, w_out_2, mix_post_g_2, xa_pre_g_2, mem_g_2, xa_wq_2, xa_wkv_2,
    xa_wo_2, xa_post_g_2, ffn2_pre_g_2, ffn2_w_gu_2, ffn2_w_down_2, ffn2_post_g_2,
):
    x = first_block(
        x, norm_pre, w_in, b_nsa_gate, cmp_pe_k, cmp_w1_k, cmp_w2_k, cmp_pe_v, cmp_w1_v,
        cmp_w2_v, w_nsa_o, w_ret_o, w_out, norm_post,
    )
    return second_block(
        x, mem_2, ffn1_pre_g_2, ffn1_w_gu_2, ffn1_w_down_2, ffn1_post_g_2, mix_pre_g_2, w_in_2,
        conv_w_2, conv_b_2, dt_bias_2, a_log_2, d_skip_2, ssd_norm_g_2, attn_norm_g_2, w_out_2,
        mix_post_g_2, xa_pre_g_2, mem_g_2, xa_wq_2, xa_wkv_2, xa_wo_2, xa_post_g_2,
        ffn2_pre_g_2, ffn2_w_gu_2, ffn2_w_down_2, ffn2_post_g_2,
    )


_drawn_inputs = setup_inputs


def setup_inputs(seed=0):
    import zlib

    import numpy as np

    out = dict(_drawn_inputs(seed))
    spreads = {}
    factors = {'b_nsa_gate': 7.661,
     'cmp_pe_k': 8.0,
     'cmp_pe_v': 8.0,
     'ffn1_pre_g_2': 5.284,
     'ffn1_post_g_2': 7.416,
     'mix_pre_g_2': 3.578,
     'conv_b_2': 4.508,
     'd_skip_2': 24.848,
     'ssd_norm_g_2': 6.818,
     'attn_norm_g_2': 7.096,
     'mix_post_g_2': 4.838,
     'xa_pre_g_2': 5.901,
     'mem_g_2': 3.881,
     'xa_post_g_2': 23.727,
     'ffn2_pre_g_2': 105.152,
     'ffn2_post_g_2': 198.532}
    for name, (base, spread) in spreads.items():
        noise = np.random.default_rng([zlib.crc32(name.encode()), seed]).standard_normal(out[name].shape)
        drawn = base * np.exp(spread * noise) if base else spread * noise
        out[name] = __import__('jax').numpy.asarray(drawn.astype(out[name].dtype))
    for name, factor in factors.items():
        out[name] = (out[name] * factor).astype(out[name].dtype)
    return out
```

```python
from contextlib import ExitStack

import numpy as np

import concourse.bass as bass
from concourse import mybir

F32 = mybir.dt.float32
F32R = mybir.dt.float32r
ACT = mybir.ActivationFunctionType
ALU = mybir.AluOpType
AX = mybir.AxisListType.X

P = 128
S = 512
SC = S // P
D = 1024
DK = D // P
FF = 2816
FK = FF // P
HALF_FK = FK // 2
EPS = 1e-6
NEG = -1e30
TINY = float(np.finfo(np.float32).tiny)

NSA_HEADS, NSA_GROUPS, DH = 8, 2, 64
NSA_PAIRS = NSA_HEADS // 2
NSA_SCALE = DH ** -0.5
CMP_LEN, CMP_STRIDE, CMP_HIDDEN = 32, 16, 256
N_CMP = (S - CMP_LEN) // CMP_STRIDE + 1
RET_HEADS, RET_DK, RET_DV = 4, 128, 256
SB_PAIRS = 8
SSD_HEADS, SSD_P, SSD_N = 16, 64, 128
CONV_K = 4
CONV_TILES = 12
MEM = 256
XA_HEADS, XA_DH = 4, 256

RAW_RING = 4
HL_RING = 2
EV_RING = 4

PARAMS = [("g_pre", DK), ("g_post", DK), ("g_ffn1_pre", DK), ("g_ffn1_post", DK), ("g_mix_pre", DK),
          ("g_attn", DK), ("g_ssd", DK), ("g_mix_post", DK), ("g_xa_pre", DK), ("g_mem", DK),
          ("g_xa_post", DK), ("g_ffn2_pre", DK), ("g_ffn2_post", DK), ("conv_b", CONV_TILES),
          ("conv_w", CONV_K * CONV_TILES), ("d_skip", DK), ("gate_b", 24), ("dt_b", SSD_HEADS),
          ("a_log", SSD_HEADS), ("pe_k", 32), ("pe_v", 32)]
PCOL = {}
_at = 0
for _n, _w in PARAMS:
    PCOL[_n] = (_at, _at + _w)
    _at += _w
NPARAM = _at

CONSTS = [("ident", P), ("ones", P), ("ones_ret", P), ("nsa_rot", P), ("causal", P), ("neg_incl", P),
          ("neg_ones", P), ("upper_incl", P), ("later", P), ("cmp_mask", SC * 32), ("cmp_keep", SC * 32)]
CCOL = {}
_at = 0
for _n, _w in CONSTS:
    CCOL[_n] = (_at, _at + _w)
    _at += _w
NCONST = _at

STAGES = [
    ("nsa_rope", 7, (8,), "ev"), ("nsa_plain", 3, (8,), "plain"), ("z_nsa", 4, (8,), "ev"),
    ("ret_rope", 8, (8,), "ev"), ("ret_v", 8, (8,), "plain"), ("z_ret", 8, (8,), "ev"),
    ("merge", 32, (8, 4, 8, 8), "ev"), ("out1", 8, (8,), "ev"),
    ("ffn1_up", 44, (8,), "ev"), ("ffn1_down", 16, (11,), "ev"),
    ("sb_qkv", 24, (8,), "plain"), ("xbc", 12, (8,), "ev"), ("z_ssd", 8, (8,), "ev"),
    ("out2", 16, (8,), "ev"), ("xa_q", 8, (8,), "plain"), ("xa_kv", 16, (8,), "plain"),
    ("xa_o", 8, (8,), "ev"), ("ffn2_up", 44, (8,), "ev"), ("ffn2_down", 16, (11,), "ev"),
]
PER_TILE = {"ffn1_down": 2, "ffn2_down": 2, "out2": 2}
SLOT0, TILE0, EV0, WIDTH, COL0 = {}, {}, {}, [], {}
_s = _t = _e = _c = 0
for _n, _k, _w, _how in STAGES:
    SLOT0[_n], TILE0[_n], EV0[_n], COL0[_n] = _s, _t, _e, _c
    WIDTH += [_w[j % len(_w)] for j in range(_k)]
    _c += sum(_w[j % len(_w)] for j in range(_k)) * P
    _s += _k
    _t += _k // PER_TILE.get(_n, 1)
    _e += _k // PER_TILE.get(_n, 1) if _how == "ev" else 0
N_SLOTS, W_COLS = _s, _c
COUNT = {n: k for n, k, _, _ in STAGES}

PRODUCTS = [("norm_pre", DK), ("z_nsa", 4), ("z_ret", 8), ("merge", 8), ("norm_ffn1", DK), ("ffn1", FK),
            ("norm_mix", DK), ("norm_attn", DK), ("norm_ssd", DK), ("norm_xa", DK), ("norm_mem", DK),
            ("xa", 8), ("norm_ffn2", DK), ("ffn2", FK)]
PROD0 = {}
_at = 0
for _n, _w in PRODUCTS:
    PROD0[_n] = _at
    _at += _w

SUMS = [("pre", DK), ("post1", 1), ("ffn1", DK), ("post_ffn1", 1), ("mix", DK), ("attn", DK), ("ssd0", 4),
        ("ssd1", 4), ("post_mix", 1), ("xa", DK), ("mem", DK), ("post_xa", 1), ("ffn2", DK), ("post_ffn2", 1)]
SUM_N, SUM_SQ0 = {}, {}
_at = 0
for _j, (_n, _w) in enumerate(SUMS):
    SUM_N[_n], SUM_SQ0[_n] = _j, _at
    _at += _w if _w > 1 else 0


BRANCH = {"out1": 0, "ffn1_down": 1, "out2": 2, "xa_o": 3, "ffn2_down": 4}
POST = {"post1": 0, "post_ffn1": 1, "post_mix": 2, "post_xa": 3, "post_ffn2": 4}
GROUP = {"merge": 8}


def run_stage(eng, name, body):
    base, n, g = SLOT0[name], COUNT[name], GROUP.get(name, 4)
    same = base + n < N_SLOTS and WIDTH[base + n] == WIDTH[base] and n % g == 0
    loops = n // g - (0 if same else 1)
    done = 0
    if loops >= 2 and base >= RAW_RING:
        with eng.Fori(0, loops) as i:
            for s in range(g):
                body(s, i, g)
        done = loops * g
    for s in range(done, n):
        body(s, 0, g)


def wait_apart(eng, sem, value, seen):
    eng.wait_ge(sem, value)
    eng.sem_inc(seen, 1)


def row(tensor, k):
    return tensor[:, bass.ds(k, 1), :].rearrange("p a s -> p (a s)")


class Tally:

    def __init__(self, eng, sem):
        self.eng, self.sem, self.base, self.k, self.i, self.per = eng, sem, 0, 0, None, 0

    def enter(self, i, per):
        self.base += self.k
        self.k, self.i, self.per = 0, i, per

    def leave(self, trips):
        assert self.k == self.per, (self.k, self.per)
        self.base += trips * self.per
        self.k, self.i = 0, None

    def link(self, ins):
        ins.then_inc(self.sem, 1)
        self.k += 1
        value = self.base + self.k
        self.eng.wait_ge(self.sem, value if self.i is None else self.i * self.per + value)


def block_program(nc, xT, mem_t, w_all, params, consts, rope, decay, w_gate, w_dt, w1k, w1v, w2k, w2v, out_t):
    ctx = ExitStack()
    with ctx:
        sems = {}

        def sem(name):
            if name not in sems:
                sems[name] = ctx.enter_context(nc.semaphore(name))
            return sems[name]

        def sb(name, shape, dt=F32):
            return ctx.enter_context(nc.sbuf_tensor(name, shape, dt))

        X = sb("residual", [P, DK, S])
        SLOT = HALF_FK * P
        WR = sb("w_raw", [P, RAW_RING, SLOT])
        WH = sb("w_hi", [P, HL_RING, SLOT], F32R)
        WL = sb("w_lo", [P, HL_RING, SLOT], F32R)
        EV = sb("evacuated", [P, EV_RING, S])
        PR = sb("product", [P, 2, S])
        SSQ = sb("square_sum", [P, S])
        RM = sb("root_mean", [P, S])
        RS = sb("rstd", [P, S])
        PA = sb("param_cols", [P, NPARAM])
        CO = sb("const_cols", [P, NCONST])
        arena0 = nc.sbuf_base
        arena_end = nc.sbuf_usable_end

        def place(name, shape, off, dt=F32):
            size = int(np.prod(shape[1:])) * 4
            assert arena0 + off * 1024 + size <= arena_end, (name, off, size, (arena_end - arena0) / 1024)
            return nc.alloc_sbuf_tensor_at(name, shape, dt, offset=arena0 + int(off * 1024))

        def par(name, j=0, n=1):
            a = PCOL[name][0] + j
            return PA[:, a:a + n]

        def const(name):
            return CO[:, CCOL[name][0]:CCOL[name][1]]

        ACC = [ctx.enter_context(nc.psum_tensor(f"acc{b}", [P, S], F32)) for b in range(2)]
        PS = [ctx.enter_context(nc.psum_tensor(f"bank{b}", [P, S], F32)) for b in range(6)]

        HH = place("act_hi", [P, DK, S], 0, F32R)
        HL = place("act_lo", [P, DK, S], 16, F32R)
        FO = place("branch_out", [P, DK, S], 0)
        TA = place("tmp_a", [P, S], 115)
        TB = place("tmp_b", [P, S], 117)
        SQ = place("squares", [P, 2, S], 119)
        QK = place("nsa_qk", [P, 7, S], 32)
        VN = place("nsa_v", [P, 3, S], 46)
        ROPE_N = place("nsa_rope_table", [P, 2, S], 52)
        ROPE_R = place("ret_rope_table", [P, 2, S], 56)
        W1 = {"k": place("cmp_w1_k", [P, 16, CMP_HIDDEN], 60), "v": place("cmp_w1_v", [P, 16, CMP_HIDDEN], 76)}
        BLK = {"k": place("cmp_blocks_k", [P, 16, 2 * N_CMP], 92), "v": place("cmp_blocks_v", [P, 16, 2 * N_CMP], 96)}
        HG = {"k": place("cmp_hidden_k", [P, 2, 2 * N_CMP], 100), "v": place("cmp_hidden_v", [P, 2, 2 * N_CMP], 100.5)}
        W2 = {"k": place("cmp_w2_k", [P, 2, DH], 101), "v": place("cmp_w2_v", [P, 2, DH], 101.5)}
        KCT = place("cmp_keys", [P, 32], 102)
        VCT = place("cmp_values", [P, 2, DH], 102.25)
        VS = place("sel_values", [P, SC, P], 103)
        VW = place("win_values", [P, SC, P], 105)
        GT = place("nsa_gates", [P, SC, 24], 107)
        WGR = place("gate_w_raw", [P, DK, 24], 108)
        WGH = place("gate_w_hi", [P, DK, 24], 109, F32R)
        WGL = place("gate_w_lo", [P, DK, 24], 110, F32R)
        QST = place("nsa_q_stage", [P, S], 60)
        PB = place("nsa_probs", [P, 2 * S + 32], 62)
        PTS = place("sel_probs_t", [P, SC, P], 67)
        PTW = place("win_probs_t", [P, SC, P], 69)
        PTC = place("cmp_probs_t", [P, P], 71)
        MX = place("nsa_max", [P, 4], 72)
        NM = place("nsa_neg_max", [P, 4], 72.25)
        SU = place("nsa_sums", [P, 4], 72.5)
        SR = place("nsa_sum_recip", [P, 4], 72.75)
        SW = place("nsa_weights", [P, 4], 73)
        OA = place("nsa_out", [P, 4, S], 74)
        GAH = place("nsa_gated_hi", [P, 4, S], 83, F32R)
        GAL = place("nsa_gated_lo", [P, 4, S], 91, F32R)
        RQK = place("ret_qk", [P, 8, S], 32)
        RSM = place("ret_scores", [P, SC, S], 48)
        RQS = place("ret_q_stage", [P, S], 56)
        RKS = place("ret_k_stage", [P, S], 58)
        RVT = place("ret_v_tokens", [P, SC, RET_DV], 60)
        RDEC = place("ret_decay", [P, S], 64)
        RV = place("ret_v", [P, 8, S], 67)
        ORT = place("ret_out", [P, 8, S], 99)
        GRH = place("ret_gated_hi", [P, 8, S], 32, F32R)
        GRL = place("ret_gated_lo", [P, 8, S], 48, F32R)
        MGL = place("merged_lo", [P, 8, S], 64, F32R)
        MGH = place("merged_hi", [P, 8, S], 99, F32R)
        AH = place("ffn_hi", [P, FK, S], 32, F32R)
        AL = place("ffn_lo", [P, FK, S], 76, F32R)
        QKV = place("sb_qkv", [P, 24, S], 32)
        OSB = place("sb_out", [P, 8, S], 80)
        BQS = place("sb_q_stage", [P, S], 96)
        BKS = place("sb_k_stage", [P, S], 98)
        BVS = place("sb_v_stage", [P, S], 100)
        BVT = place("sb_v_tokens", [P, SC, P], 102)
        SPB = place("sb_softplus", [P, 5, S], 104)
        OSH = place("sb_hi", [P, 8, S], 32, F32R)
        OSL = place("sb_lo", [P, 8, S], 48, F32R)
        XBC = place("ssd_xbc", [P, CONV_TILES, S], 64)
        BTK = place("ssd_b_tokens", [P, 2, SC, P], 88)
        CBM = place("ssd_cb", [P, 2, SC, P], 92)
        XST = EV[:, 1, :]
        X1 = place("ssd_x_dt", [P, SC, 2, SSD_P], 98)
        X2 = place("ssd_x_decayed", [P, SC, 2, SSD_P], 100)
        LSG = place("ssd_segments", [P, SC, 2, P], 102)
        LM = place("ssd_decays", [P, 2, SC, P], 106)
        ARP = place("ssd_adt_rows", [P, SC, P], 110)
        ERW = EV[:, 0, :]
        STT_ = place("ssd_states", [P, 3, P], 112)
        WDR = place("dt_w_raw", [P, DK, SSD_HEADS], 106)
        WDH = place("dt_w_hi", [P, DK, SSD_HEADS], 107, F32R)
        WDL = place("dt_w_lo", [P, DK, SSD_HEADS], 108, F32R)
        DTX = place("dt_in", [P, SC, SSD_HEADS], 113.5)
        DTL = place("dt_log", [P, SC, SSD_HEADS], 113.75)
        DT = place("dt", [P, SC, SSD_HEADS], 114)
        ADT = place("a_dt", [P, SC, SSD_HEADS], 114.25)
        DEND = place("decay_to_end", [P, SC, SSD_HEADS], 114.5)
        CDEC = place("chunk_decay", [P, SC, SSD_HEADS], 114.75)
        EAL = place("a_exp", [P, SSD_HEADS], 96)
        YSH = place("ssd_hi", [P, 8, S], 80, F32R)
        YSL = place("ssd_lo", [P, 8, S], 96, F32R)
        XQ = place("xa_q", [P, 8, S], 32)
        XKV = place("xa_kv", [P, 16, MEM], 48)
        MR = place("mem_raw", [P, DK, MEM], 64)
        MH = place("mem_hi", [P, DK, MEM], 72, F32R)
        ML = place("mem_lo", [P, DK, MEM], 80, F32R)
        XOH = place("xa_hi", [P, 8, S], 72, F32R)
        XOL = place("xa_lo", [P, 8, S], 88, F32R)
        CQS = place("xa_q_stage", [P, 2, S], 64)
        CKS = place("xa_k_stage", [P, 2, MEM], 68)
        CVS = place("xa_v_stage", [P, 2, MEM], 70)
        CVT = place("xa_v_tokens", [P, 2, XA_DH], 104)
        CP = place("xa_probs", [P, SC, MEM], 106)
        CPT = place("xa_probs_t", [P, 2, S], 110)
        CMX = place("xa_max", [P, SC], 114)
        CNM = place("xa_neg_max", [P, SC], 114.25)
        CSU = place("xa_sums", [P, SC], 114.5)
        CSR = place("xa_sum_recip", [P, SC], 114.75)

        ident, ones, ones_ret = const("ident"), const("ones"), const("ones_ret")
        s_in = sem("inputs_landed")
        s_xin = sem("x_landed")
        s_late = {n: sem(n + "_landed") for n in ("cmp_w", "rope_ret", "decay", "mem", "dt_w")}
        s_raw = [sem(f"w_landed{r}") for r in range(RAW_RING)]
        s_hi, s_lo, s_used = sem("w_hi_ready"), sem("w_lo_ready"), sem("w_slot_used")
        s_acc = sem("acc_evacuated")
        s_sq, s_squsd = sem("square_ready"), sem("square_summed")
        s_psum, s_root, s_rstd = sem("post_summed"), sem("root_ready"), sem("rstd_ready")
        s_pr, s_ph, s_pl = sem("product_ready"), sem("product_hi"), sem("product_lo")
        s_x = sem("residual_updated")
        s_fsq = sem("branch_square_added")
        s_out = sem("out_stored")
        s_dch = sem("dve_chain")
        block = ctx.enter_context(nc.Block())

        def sb_tmp(b):
            return EV[:, b, :] if b < EV_RING else TA[:]

        @block.sync
        def _(sp):
            sp.dma_start(CO[:], consts).then_inc(s_in, 16)
            sp.dma_start(PA[:], params).then_inc(s_in, 16)
            sp.dma_start(ROPE_N[:], rope[:, 0:2, :]).then_inc(s_in, 16)
            sp.dma_start(WGR[:], w_gate).then_inc(s_in, 16)
            sp.dma_start(X[:], xT).then_inc(s_xin, 16)

            def load_stage(name):
                base, wide = SLOT0[name], sum(WIDTH[SLOT0[name]:SLOT0[name] + GROUP.get(name, 4)]) * P

                def body(s, i, g):
                    c = base + s
                    col = COL0[name] + sum(WIDTH[base:c]) * P
                    if c >= RAW_RING:
                        sp.wait_ge(s_lo, i * g + c - RAW_RING + 1)
                    sp.dma_start(WR[:, c % RAW_RING, 0:WIDTH[c] * P],
                                 w_all[:, bass.ds(i * wide + col, WIDTH[c] * P)]).then_inc(s_raw[c % RAW_RING], 16)
                run_stage(sp, name, body)

            load_stage("nsa_rope")
            for t in ("k", "v"):
                sp.dma_start(W1[t][:], w1k if t == "k" else w1v).then_inc(s_late["cmp_w"], 16)
                sp.dma_start(W2[t][:], w2k if t == "k" else w2v).then_inc(s_late["cmp_w"], 16)
            sp.dma_start(ROPE_R[:], rope[:, 2:4, :]).then_inc(s_late["rope_ret"], 16)
            for name in ("nsa_plain", "z_nsa", "ret_rope", "ret_v", "z_ret", "merge", "out1", "ffn1_up",
                         "ffn1_down", "sb_qkv", "xbc", "z_ssd", "out2", "xa_q", "xa_kv", "xa_o", "ffn2_up",
                         "ffn2_down"):
                load_stage(name)
            for k in range(DK):
                sp.wait_ge(s_x, 4 * DK + k + 1)
                sp.dma_start(out_t[:, k, :], X[:, k, :]).then_inc(s_out, 16)
            sp.wait_ge(s_out, 16 * DK)

        @block.gpsimd
        def _(pool):
            pool.wait_ge(sem("nsa_out"), NSA_PAIRS)
            pool.dma_start(RDEC[:], decay[:, 0, :]).then_inc(s_late["decay"], 16)
            with pool.Fori(1, RET_HEADS) as h:
                pool.wait_ge(sem("ret_decayed"), h * SC)
                pool.dma_start(RDEC[:], row(decay, h)).then_inc(s_late["decay"], 16)

            def keep_later(view, op, blocks):
                return nc.gpsimd.affine_select(out=view, in_=view, compare_op=op, fill=0.0, base=0,
                                               pattern=[[0, blocks], [1, P]], channel_multiplier=-1)

            def diagonals(tile, b):
                v = tile.rearrange("p (a c) -> p a c", c=P)
                return v[:, 0:1, :] if b < 2 else v[:, 0:4:3, :] if b < 4 else v[:, 0:4:2, :]

            with pool.Fori(0, SB_PAIRS) as p:
                for b in range(5):
                    wait_apart(pool, sem("sb_softplus"), p * 5 + b + 1, sem("pool_seen"))
                    keep_later(diagonals(SPB[:, b, :], b), ALU.is_gt, 1 if b < 2 else 2).then_inc(
                        sem("sb_softplus_masked"), 1)
                for b in range(5):
                    wait_apart(pool, sem("sb_exp"), p * 5 + b + 1, sem("pool_seen"))
                    keep_later(diagonals(sb_tmp(b), b), ALU.is_gt, 1 if b < 2 else 2).then_inc(
                        sem("sb_exp_masked"), 1)
            pool.wait_ge(sem("sb_out"), SB_PAIRS)
            pool.dma_start(WDR[:], w_dt).then_inc(s_late["dt_w"], 16)
            for g in range(2):
                pool.wait_ge(sem("ssd_cb"), g + 1)
                keep_later(CBM[:, g], ALU.is_ge, SC).then_inc(sem("ssd_cb_masked"), 1)
            pool.wait_ge(s_x, 3 * DK)
            pool.dma_start(MR[:], mem_t).then_inc(s_late["mem"], 16)


        @block.scalar
        def _(act):
            A = nc.scalar.activation
            nc.scalar.sem_inc(sem("conv_silu"), 1)

            def split_hi(c, i, g):
                nb = WIDTH[c]
                act.wait_ge(s_raw[c % RAW_RING], i * (16 * g // 4) + 16 * (c // RAW_RING + 1))
                if c >= HL_RING:
                    act.wait_ge(s_used, i * g + c - HL_RING + 1)
                A(WH[:, c % HL_RING, 0:nb * P], WR[:, c % RAW_RING, 0:nb * P], ACT.Copy).then_inc(s_hi, 1)

            def stage(name, tile):
                base, per = SLOT0[name], PER_TILE.get(name, 1)

                def body(s, i, g):
                    if base + s + 1 < N_SLOTS:
                        split_hi(base + s + 1, i, g)
                    if s % per == per - 1:
                        act.wait_ge(s_used, i * g + base + s + 1)
                        tile(s // per, i, g // per)
                run_stage(act, name, body)

            def acc(name, t):
                return ACC[(TILE0[name] + t) % 2][:]

            def ev(name, t):
                return EV[:, (EV0[name] + t) % EV_RING, :]

            def squares(name, src, ready, n=S):
                q0 = SUM_SQ0[name]
                for k in range(SUMS[SUM_N[name]][1]):
                    ready(k)
                    if q0 + k >= 2:
                        act.wait_ge(s_squsd, q0 + k - 1)
                    A(SQ[:, (q0 + k) % 2, 0:n], src(k), ACT.Square).then_inc(s_sq, 1)

            def root(name, dim, n=S):
                j = SUM_N[name]
                if SUMS[j][1] > 1:
                    act.wait_ge(s_squsd, SUM_SQ0[name] + SUMS[j][1])
                else:
                    act.wait_ge(s_psum, POST[name] + 1)
                if j:
                    act.wait_ge(s_rstd, j)
                A(RM[:, 0:n], PS[5][:, 0:n], ACT.Sqrt, scale=1.0 / dim, bias=EPS).then_inc(s_root, 1)

            def product_hi(j, off, dst, n=S):
                act.wait_ge(s_pr, off + j + 1)
                A(dst, PR[:, j % 2, 0:n], ACT.Copy).then_inc(s_ph, 1)

            def norm_hi(name, dst, n=S, ks=range(DK)):
                for k in ks:
                    product_hi(PROD0[name] + k, 0, dst(k), n)

            def boundary(b, post, pre, prod):
                root(post, D)
                squares(pre, lambda k: X[:, k, :], lambda k: act.wait_ge(s_x, b * DK + k + 1))
                root(pre, D)
                norm_hi(prod, lambda k: HH[:, k, :])

            def branch(name):
                def tile(t, i, m):
                    A(row(FO, i * m + t), acc(name, t), ACT.Copy)
                    act.wait_ge(s_fsq, i * m + BRANCH[name] * DK + t + 1)
                    A(ev(name, t), acc(name, t), ACT.Square).then_inc(s_acc, 1)
                stage(name, tile)

            def plain(name, dst, n=S):
                stage(name, lambda t, i, m: A(row(dst, i * m + t), acc(name, t)[:, 0:n], ACT.Copy).then_inc(s_acc, 1))

            def gated(name, dst_hi):
                def tile(t, i, m):
                    A(ev(name, t), acc(name, t), ACT.Silu).then_inc(s_acc, 1)
                    product_hi(PROD0[name] + t, i * m, row(dst_hi, i * m + t))
                stage(name, tile)

            act.wait_ge(s_in, 64)
            A(WGH[:], WGR[:], ACT.Copy).then_inc(sem("gate_w_hi"), 1)
            act.wait_ge(s_xin, 16)
            squares("pre", lambda k: X[:, k, :], lambda k: None)
            root("pre", D)
            norm_hi("norm_pre", lambda k: HH[:, k, :])
            split_hi(0, 0, 4)

            def nsa_rope_tile(t, i, m):
                if t >= EV_RING:
                    act.wait_ge(sem("nsa_roped"), t - EV_RING + 1)
                A(ev("nsa_rope", t), acc("nsa_rope", t), ACT.Copy).then_inc(s_acc, 1)
            stage("nsa_rope", nsa_rope_tile)
            plain("nsa_plain", VN)

            act.wait_ge(sem("gate_sum"), 1)
            A(GT[:], GT[:], ACT.Sigmoid).then_inc(sem("gate_ready"), 1)
            for n, t in enumerate(("k", "v")):
                act.wait_ge(sem("cmp_hidden"), n + 1)
                A(HG[t][:], PS[n][:, 0:4 * N_CMP].rearrange("p (j c) -> p j c", j=2),
                  ACT.Gelu_apprx_tanh).then_inc(sem("cmp_gelu"), 1)

            with act.Fori(0, NSA_PAIRS) as p:
                for u in range(8):
                    kw = (u // 2 + 1) * P
                    act.wait_ge(sem("nsa_max"), p * 8 + u + 1)
                    A(PB[:, 0:kw], PS[0][:, 0:kw], ACT.Exp, bias=NM[:, 1:2], scale=NSA_SCALE, accum_out=SU[:, 1:2])
                    A(PB[:, S:S + kw], PS[1][:, 0:kw], ACT.Exp, bias=NM[:, 2:3], scale=NSA_SCALE,
                      accum_out=SU[:, 2:3])
                    A(PB[:, 2 * S:2 * S + N_CMP], PS[2][:, 0:N_CMP], ACT.Exp, bias=NM[:, 0:1],
                      scale=NSA_SCALE).then_inc(sem("nsa_exp"), 1)
                    act.wait_ge(sem("nsa_turned"), p * 8 + u + 1)
                    A(PTS[:, 0:kw // P, :], PS[3][:, 0:kw].rearrange("p (c t) -> p c t", t=P),
                      ACT.Copy).then_inc(sem("nsa_sel_t"), 1)
                act.wait_ge(sem("nsa_pv"), p * 8 + 8)
                A(row(OA, p), PS[5][:], ACT.Copy).then_inc(sem("nsa_out"), 1)
            gated("z_nsa", GAH)

            def ret_rope_tile(t, i, m):
                act.wait_ge(sem("ret_roped"), i * m + t + 1)
                A(ev("ret_rope", t), acc("ret_rope", t), ACT.Copy).then_inc(s_acc, 1)
            stage("ret_rope", ret_rope_tile)
            plain("ret_v", RV)
            act.wait_ge(sem("ret_roped"), EV_RING + 8)
            with act.Fori(0, RET_HEADS) as h:
                A(EV[:, 0:2, :], RV[:, bass.ds(h * 2, 2), :], ACT.Copy).then_inc(sem("ret_v_staged"), 1)
                act.wait_ge(sem("ret_pv"), h + 1)
                for e in range(2):
                    A(row(ORT, h * 2 + e), PS[3 + e][:], ACT.Copy).then_inc(sem("ret_raw"), 1)
                for e in range(2):
                    wait_apart(act, sem("ret_centred"), h * 2 + e + 1, sem("act_seen"))
                    A(EV[:, 2 + e, :], row(ORT, h * 2 + e), ACT.Square).then_inc(sem("ret_sq"), 1)
                act.wait_ge(sem("ret_var"), h + 1)
                A(TA[:], PS[1][:], ACT.Sqrt, bias=EPS).then_inc(sem("ret_root"), 1)
            gated("z_ret", GRH)

            def merge_tile(t, i, m):
                A(ev("merge", t), acc("merge", t), ACT.Copy if t % 2 else ACT.Sigmoid).then_inc(s_acc, 1)
                if t % 4 == 3:
                    product_hi(PROD0["merge"] + t // 4, i * 2, row(MGH, i * 2 + t // 4))
            stage("merge", merge_tile)
            branch("out1")
            boundary(0, "post1", "ffn1", "norm_ffn1")

            def ffn(n):
                up = f"ffn{n}_up"

                def tile(t, i, m):
                    A(ev(up, t), acc(up, t), ACT.Copy if t % 2 else ACT.Silu).then_inc(s_acc, 1)
                    if t % 2:
                        product_hi(PROD0[f"ffn{n}"] + t // 2, i * 2, row(AH, i * 2 + t // 2))
                stage(up, tile)
                branch(f"ffn{n}_down")
            ffn(1)
            boundary(1, "post_ffn1", "mix", "norm_mix")

            plain("sb_qkv", QKV)
            with act.Fori(0, SB_PAIRS) as p:
                for b in range(5):
                    act.wait_ge(sem("sb_scored"), p * 5 + b + 1)
                    A(sb_tmp(b), PS[b][:], ACT.Abs).then_inc(sem("sb_abs"), 1)
                for b in range(5):
                    act.wait_ge(sem("sb_abs"), p * 5 + b + 1)
                    A(sb_tmp(b), sb_tmp(b), ACT.Exp, scale=-1.0).then_inc(sem("sb_neg_exp"), 1)
                    act.wait_ge(sem("sb_neg_exp"), p * 5 + b + 1)
                    A(sb_tmp(b), sb_tmp(b), ACT.Ln, bias=1.0).then_inc(sem("sb_log"), 1)
                for b in range(5):
                    act.wait_ge(sem("sb_suffixed"), p * 5 + b + 1)
                    A(sb_tmp(b), PS[b][:], ACT.Exp).then_inc(sem("sb_exp"), 1)
                act.wait_ge(sem("sb_pv"), p + 1)
                A(row(OSB, p), PS[5][:], ACT.Copy).then_inc(sem("sb_out"), 1)
            squares("attn", lambda k: OSB[:, k, :], lambda k: act.wait_ge(sem("sb_out"), SB_PAIRS))
            root("attn", D)
            norm_hi("norm_attn", lambda k: OSH[:, k, :])

            def xbc_tile(t, i, m):
                A(ev("xbc", t), acc("xbc", t), ACT.Copy).then_inc(s_acc, 1)
                act.wait_ge(sem("conv_sum"), i * m + t + 1)
                A(row(XBC, i * m + t), TB[:], ACT.Silu).then_inc(sem("conv_silu"), 1)
            stage("xbc", xbc_tile)
            act.wait_ge(s_late["dt_w"], 16)
            A(WDH[:], WDR[:], ACT.Copy).then_inc(sem("dt_w_hi"), 1)
            A(EAL[:], par("a_log", 0, SSD_HEADS), ACT.Exp).then_inc(sem("a_exp"), 1)
            act.wait_ge(sem("dt_in"), 1)
            A(DTL[:], DTX[:], ACT.Abs).then_inc(sem("dt_log"), 1)
            act.wait_ge(sem("dt_log"), 1)
            A(DTL[:], DTL[:], ACT.Exp, scale=-1.0).then_inc(sem("dt_log"), 1)
            act.wait_ge(sem("dt_log"), 2)
            A(DTL[:], DTL[:], ACT.Ln, bias=1.0).then_inc(sem("dt_log"), 1)
            act.wait_ge(sem("dt_sums"), 1)
            A(DEND[:], PS[1][:, 0:64].rearrange("p (c h) -> p c h", c=SC), ACT.Exp)
            A(CDEC[:], PS[2][:, 0:64].rearrange("p (c h) -> p c h", c=SC), ACT.Exp).then_inc(sem("dt_decays"), 1)
            for g in range(2):
                act.wait_ge(sem("ssd_bt"), g + 1)
                A(BTK[:, g], PS[3 + g][:].rearrange("p (c n) -> p c n", c=SC), ACT.Copy).then_inc(sem("ssd_b_tokens"), 1)
            for g in range(2):
                with act.Fori(0, 4) as p:
                    act.wait_ge(sem("ssd_seg"), p + 4 * g + 1)
                    for hh in range(2):
                        A(LM[:, hh], PS[1 + hh][:].rearrange("p (c t) -> p c t", c=SC), ACT.Exp).then_inc(
                            sem("ssd_seg_exp"), 1)
                    act.wait_ge(sem("ssd_rows"), p + 4 * g + 1)
                    A(ERW[:, P:S], PS[3][:, P:S], ACT.Exp).then_inc(sem("ssd_row_exp"), 1)

            def z_ssd_tile(t, i, m):
                act.wait_ge(sem("ssd_gated"), i * m + t + 1)
                A(ev("z_ssd", t), acc("z_ssd", t), ACT.Silu).then_inc(s_acc, 1)
            stage("z_ssd", z_ssd_tile)
            for g in range(2):
                squares(f"ssd{g}", lambda k: XBC[:, 4 * g + k, :], lambda k: act.wait_ge(sem("ssd_gated"), 12))
                root(f"ssd{g}", D // 2)
                norm_hi("norm_ssd", lambda k: YSH[:, k, :], ks=range(4 * g, 4 * g + 4))
            branch("out2")
            boundary(2, "post_mix", "xa", "norm_xa")

            plain("xa_q", XQ)
            act.wait_ge(s_late["mem"], 16)
            squares("mem", lambda k: MR[:, k, :], lambda k: None, MEM)
            root("mem", D, MEM)
            norm_hi("norm_mem", lambda k: MH[:, k, :], MEM)
            plain("xa_kv", XKV, MEM)
            with act.Fori(0, XA_HEADS) as h:
                act.wait_ge(sem("xa_max"), h + 1)
                for i in range(SC):
                    A(CP[:, i, :], PS[1 + i // 2][:, (i % 2) * MEM:(i % 2 + 1) * MEM], ACT.Exp,
                      bias=CNM[:, i:i + 1], scale=XA_DH ** -0.5, accum_out=CSU[:, i:i + 1]).then_inc(sem("xa_exp"), 1)
                for mc in range(2):
                    act.wait_ge(sem("xa_turned"), h * 2 + mc + 1)
                    A(CPT[:, mc, :], PS[3 + mc][:], ACT.Copy).then_inc(sem("xa_probs_t"), 1)
                for e in range(2):
                    product_hi(PROD0["xa"] + e, h * 2, row(XOH, h * 2 + e))
            branch("xa_o")
            boundary(3, "post_xa", "ffn2", "norm_ffn2")
            ffn(2)
            root("post_ffn2", D)

        @block.vector
        def _(dve):
            V = nc.vector
            TT, TS, STT = V.tensor_tensor, V.tensor_scalar, V.scalar_tensor_tensor
            chain = Tally(dve, s_dch)
            V.sem_inc(s_fsq, EV_RING)
            V.sem_inc(sem("ret_roped"), EV_RING)
            V.sem_inc(sem("ssd_gated"), EV_RING)

            def split_lo(c, i, g):
                nb = WIDTH[c]
                dve.wait_ge(s_hi, i * g + c + 1)
                TT(WL[:, c % HL_RING, 0:nb * P], WR[:, c % RAW_RING, 0:nb * P],
                   WH[:, c % HL_RING, 0:nb * P].bitcast(F32), ALU.subtract).then_inc(s_lo, 1)

            def stage(name, tile=None, per=None):
                base, per = SLOT0[name], per or PER_TILE.get(name, 1)

                def body(s, i, g):
                    if base + s + 1 < N_SLOTS:
                        split_lo(base + s + 1, i, g)
                    if tile is not None and s % per == per - 1:
                        tiles = g // PER_TILE.get(name, 1)
                        t = s // PER_TILE.get(name, 1)
                        dve.wait_ge(s_acc, i * tiles + TILE0[name] + t + 1)
                        tile(s // per, i, g // per)
                run_stage(dve, name, body)

            def ev(name, t):
                return EV[:, (EV0[name] + t) % EV_RING, :]

            def free_product(j, off):
                if j >= 2:
                    dve.wait_ge(s_pl, off + j - 1)

            def low(j, off, hi, lo, n=S):
                dve.wait_ge(s_ph, off + j + 1)
                TT(lo, PR[:, j % 2, 0:n], hi.bitcast(F32), ALU.subtract).then_inc(s_pl, 1)

            def rstd(name, n=S):
                j = SUM_N[name]
                dve.wait_ge(s_root, j + 1)
                V.reciprocal(RS[:, 0:n], RM[:, 0:n]).then_inc(s_rstd, 1)
                dve.wait_ge(s_rstd, j + 1)

            def apply_norm(name, src, gain, hi, lo, n=S, ks=range(DK)):
                def make(k):
                    j = PROD0[name] + k
                    free_product(j, 0)
                    STT(out=PR[:, j % 2, 0:n], in0=src(k), scalar=par(gain, k), in1=RS[:, 0:n], op0=ALU.mult,
                        op1=ALU.mult).then_inc(s_pr, 1)
                make(ks[0])
                for k in ks:
                    if k + 1 in ks:
                        make(k + 1)
                    low(PROD0[name] + k, 0, hi(k), lo(k), n)

            def norm(total, name, gain):
                rstd(total)
                apply_norm(name, lambda k: X[:, k, :], gain, lambda k: HH[:, k, :], lambda k: HL[:, k, :])

            def branch(name):
                def add_square(t, i, m):
                    TT(SSQ[:], SSQ[:], ev(name, t), ALU.add).then_inc(s_fsq, 1)
                    dve.wait_ge(s_fsq, i * m + BRANCH[name] * DK + EV_RING + t + 1)
                chain.link(V.memset(SSQ[:], 0.0))
                stage(name, add_square)

            def boundary(b, post, gain, factor):
                rstd(post)
                for k in range(DK):
                    t = (TA, TB)[k % 2]
                    chain.link(STT(out=t[:], in0=FO[:, k, :], scalar=par(gain, k), in1=RS[:], op0=ALU.mult, op1=ALU.mult))
                    STT(out=X[:, k, :], in0=t[:], scalar=factor, in1=X[:, k, :], op0=ALU.mult, op1=ALU.add).then_inc(s_x, 1)

            def gated(name, src, lo, hi):
                def tile(t, i, m):
                    j = PROD0[name] + t
                    free_product(j, i * m)
                    TT(PR[:, j % 2, :], ev(name, t), row(src, i * m + t), ALU.mult).then_inc(s_pr, 1)
                    low(j, i * m, row(hi, i * m + t), row(lo, i * m + t))
                stage(name, tile)

            dve.wait_ge(sem("gate_w_hi"), 1)
            TT(WGL[:], WGR[:], WGH[:].bitcast(F32), ALU.subtract).then_inc(sem("gate_w_lo"), 1)
            norm("pre", "norm_pre", "g_pre")
            split_lo(0, 0, 4)

            def nsa_rope_tile(t, i, m):
                chain.link(TT(TB[:], ev("nsa_rope", t), ROPE_N[:, 0, :], ALU.mult))
                dve.wait_ge(sem("nsa_turned_half"), t + 1)
                chain.link(TT(TA[:], PS[t % 2][:], ROPE_N[:, 1, :], ALU.mult))
                TT(QK[:, t, :], TA[:], TB[:], ALU.add).then_inc(sem("nsa_roped"), 1)
                dve.wait_ge(sem("nsa_roped"), t + 1)
            stage("nsa_rope", nsa_rope_tile)
            stage("nsa_plain")

            dve.wait_ge(sem("gate_psum"), 1)
            TT(GT[:], PS[2][:, 0:SC * 24].rearrange("p (c h) -> p c h", c=SC),
               par("gate_b", 0, 24).unsqueeze(1).broadcast_to([P, SC, 24]), ALU.add).then_inc(sem("gate_sum"), 1)
            for n, dst in enumerate((VS, VW)):
                dve.wait_ge(sem("nsa_v_turned"), n + 1)
                V.tensor_copy(dst[:], PS[3 + n][:].rearrange("p (c f) -> p c f", c=SC)).then_inc(sem("nsa_v_tokens"), 1)
            for t, src in (("k", QK[:, 4, :]), ("v", VN[:, 0, :])):
                if t == "v":
                    dve.wait_ge(s_acc, TILE0["nsa_plain"] + 3)
                for g in range(2):
                    kv = src[64 * g:64 * g + 64, :].rearrange("p (m b r) -> p m b r", b=8, r=2)
                    for r in range(2):
                        for a in range(2):
                            pe_at = PCOL["pe_" + t][0] + r * 16 + a * 8
                            last = TT(BLK[t][64 * r:64 * r + 64, 8 * a:8 * a + 8, g * N_CMP:(g + 1) * N_CMP],
                                      kv[:, a:a + N_CMP, :, r].rearrange("p m b -> p b m"),
                                      PA[64 * g:64 * g + 64, pe_at:pe_at + 8].unsqueeze(2).broadcast_to(
                                          [64, 8, N_CMP]), ALU.add)
                last.then_inc(sem("cmp_blocks"), 1)
            dve.wait_ge(sem("cmp_done"), 1)
            V.tensor_copy(KCT[:, 0:N_CMP], PS[2][:, 0:N_CMP])
            V.tensor_copy(VCT[0:N_CMP, :, :], PS[2][0:N_CMP, P:2 * P].rearrange("p (g d) -> p g d", g=2)).then_inc(
                sem("cmp_kv"), 1)

            with dve.Fori(0, NSA_PAIRS) as p:
                chain.enter(p, 8 * 6)
                V.tensor_copy(QST[:], row(QK, p)).then_inc(sem("nsa_staged"), 1)
                for u in range(8):
                    i, hh = divmod(u, 2)
                    kw = (i + 1) * P
                    dve.wait_ge(sem("nsa_scored"), p * 8 + u + 1)
                    V.reduce_max(MX[:, 1:2], PS[0][:, 0:kw], AX)
                    V.reduce_max(MX[:, 2:3], PS[1][:, 0:kw], AX)
                    chain.link(V.reduce_max(MX[:, 0:1], PS[2][:, 0:N_CMP], AX))
                    TS(NM[:, 0:3], MX[:, 0:3], -NSA_SCALE, None, ALU.mult).then_inc(sem("nsa_max"), 1)
                    dve.wait_ge(sem("nsa_exp"), p * 8 + u + 1)
                    pc = PB[:, 2 * S:2 * S + N_CMP]
                    keep = const("cmp_keep")[:, i * 32:i * 32 + N_CMP]
                    chain.link(TT(pc, pc, keep, ALU.mult))
                    chain.link(V.reduce_sum(SU[:, 0:1], pc, AX))
                    chain.link(TS(SU[:, 0:3], SU[:, 0:3], TINY, None, ALU.max))
                    chain.link(V.reciprocal(SR[:, 0:3], SU[:, 0:3]))
                    chain.link(TT(SW[:, 0:3], SR[:, 0:3], GT[:, i, bass.ds(p * 3 + 12 * hh, 3)], ALU.mult))
                    TS(pc, pc, SW[:, 0:1], None, ALU.mult)
                    TS(PB[:, 0:kw], PB[:, 0:kw], SW[:, 1:2], None, ALU.mult)
                    TS(PB[:, S:S + kw], PB[:, S:S + kw], SW[:, 2:3], None, ALU.mult).then_inc(sem("nsa_scaled"), 1)
                    dve.wait_ge(sem("nsa_turned"), p * 8 + u + 1)
                    V.tensor_copy(PTC[0:N_CMP, :], PS[2][0:N_CMP, P:2 * P])
                    V.tensor_copy(PTW[:, 0:i + 1, :], PS[4][:, 0:kw].rearrange("p (c t) -> p c t", t=P)).then_inc(
                        sem("nsa_win_t"), 1)
                dve.wait_ge(sem("nsa_out"), p + 1)
                chain.leave(NSA_PAIRS)
            gated("z_nsa", OA, GAL, GAH)

            def ret_rope_tile(t, i, m):
                e = ev("ret_rope", t)
                TT(TA[0:64, :], e[64:128, :], ROPE_R[64:128, 1, :], ALU.mult)
                TT(TA[64:128, :], e[0:64, :], ROPE_R[0:64, 1, :], ALU.mult)
                TT(TB[:], e, ROPE_R[:, 0, :], ALU.mult).then_inc(sem("ret_rope_parts"), 1)
                dve.wait_ge(sem("ret_rope_parts"), i * m + t + 1)
                TT(row(RQK, i * m + t), TA[:], TB[:], ALU.add).then_inc(sem("ret_roped"), 1)
                dve.wait_ge(sem("ret_roped"), i * m + t + 1 + EV_RING)
            dve.wait_ge(s_late["rope_ret"], 16)
            stage("ret_rope", ret_rope_tile)
            stage("ret_v")
            with dve.Fori(0, RET_HEADS) as h:
                V.tensor_copy(RQS[:], row(RQK, h))
                V.tensor_copy(RKS[:], row(RQK, h + RET_HEADS)).then_inc(sem("ret_staged"), 1)
                for e in range(2):
                    dve.wait_ge(sem("ret_v_turned"), h * 2 + e + 1)
                    V.tensor_copy(RVT[:, :, e * P:(e + 1) * P], PS[e][:].rearrange("p (c f) -> p c f", c=SC)).then_inc(
                        sem("ret_v_tokens"), 1)
                dve.wait_ge(s_late["decay"], h * 16 + 16)
                for j in range(SC):
                    w = S - j * P
                    dve.wait_ge(sem("ret_scored"), h * SC + j + 1)
                    TT(RSM[:, j, 0:w], PS[(2, 5)[j % 2]][:, 0:w], RDEC[:, 0:w], ALU.mult).then_inc(sem("ret_decayed"), 1)
                for e in range(2):
                    o = row(ORT, h * 2 + e)
                    if e == 0:
                        dve.wait_ge(sem("ret_mean"), h + 1)
                    TT(o, o, PS[0][:], ALU.subtract).then_inc(sem("ret_centred"), 1)
                dve.wait_ge(sem("ret_root"), h + 1)
                V.reciprocal(TB[:], TA[:]).then_inc(sem("ret_rstd"), 1)
                dve.wait_ge(sem("ret_rstd"), h + 1)
                dve.wait_ge(sem("ret_centred"), h * 2 + 2)
                TT(row(ORT, h * 2), row(ORT, h * 2), TB[:], ALU.mult)
                TT(row(ORT, h * 2 + 1), row(ORT, h * 2 + 1), TB[:], ALU.mult).then_inc(sem("ret_done"), 1)
            dve.wait_ge(sem("ret_done"), RET_HEADS)
            gated("z_ret", ORT, GRL, GRH)

            def merge_tile(t, i, m):
                e = [ev("merge", 4 * t + u) for u in range(4)]
                j = PROD0["merge"] + t
                TT(TA[:], e[0], e[1], ALU.mult).then_inc(sem("merge_parts"), 1)
                TT(TB[:], e[2], e[3], ALU.mult).then_inc(sem("merge_parts"), 1)
                dve.wait_ge(sem("merge_parts"), (i * m + t) * 2 + 2)
                free_product(j, i * m)
                TT(PR[:, j % 2, :], TA[:], TB[:], ALU.add).then_inc(s_pr, 1)
                low(j, i * m, row(MGH, i * m + t), row(MGL, i * m + t))
            stage("merge", merge_tile, per=4)
            branch("out1")
            boundary(0, "post1", "g_post", 1.0)
            norm("ffn1", "norm_ffn1", "g_ffn1_pre")

            def ffn(n):
                def tile(t, i, m):
                    j = PROD0[f"ffn{n}"] + t
                    free_product(j, i * m)
                    TT(PR[:, j % 2, :], ev(f"ffn{n}_up", 2 * t), ev(f"ffn{n}_up", 2 * t + 1), ALU.mult).then_inc(s_pr, 1)
                    low(j, i * m, row(AH, i * m + t), row(AL, i * m + t))
                stage(f"ffn{n}_up", tile, per=2)
                branch(f"ffn{n}_down")
            ffn(1)
            boundary(1, "post_ffn1", "g_ffn1_post", 0.5)
            norm("mix", "norm_mix", "g_mix_pre")

            stage("sb_qkv")
            dve.wait_ge(s_acc, TILE0["xbc"])
            with dve.Fori(0, SB_PAIRS) as p:
                TS(BQS[:], row(QKV, p), DH ** -0.5, None, ALU.mult)
                V.tensor_copy(BKS[:], row(QKV, p + 8))
                V.tensor_copy(BVS[:], row(QKV, p + 16)).then_inc(sem("sb_staged"), 1)
                dve.wait_ge(sem("sb_v_turned"), p + 1)
                V.tensor_copy(BVT[:], PS[5][:].rearrange("p (c f) -> p c f", c=SC)).then_inc(sem("sb_v_tokens"), 1)
                for b in range(5):
                    dve.wait_ge(sem("sb_log"), p * 5 + b + 1)
                    STT(out=SPB[:, b, :], in0=PS[b][:], scalar=0.0, in1=sb_tmp(b), op0=ALU.max, op1=ALU.add).then_inc(
                        sem("sb_softplus"), 1)
                dve.wait_ge(sem("sb_out"), p + 1)
            rstd("attn")
            apply_norm("norm_attn", lambda k: OSB[:, k, :], "g_attn", lambda k: OSH[:, k, :], lambda k: OSL[:, k, :])

            def conv_tile(t, i, m):
                x = ev("xbc", t)

                def tap(k):
                    a = PCOL["conv_w"][0] + k * CONV_TILES
                    return PA[:, bass.ds(i * m + (a + t), 1)]
                ab = PCOL["conv_b"][0] + t
                bias = PA[:, bass.ds(i * m + ab, 1)]
                dve.wait_ge(sem("conv_silu"), i * m + t + 1)
                conv = sem("conv_chain")
                n = (i * m + t) * 3
                TS(TA[:], x, tap(3), bias, ALU.mult, ALU.add).then_inc(conv, 1)
                dve.wait_ge(conv, n + 1)
                STT(out=TA[:, 1:S], in0=x[:, 0:S - 1], scalar=tap(2), in1=TA[:, 1:S], op0=ALU.mult, op1=ALU.add).then_inc(conv, 1)
                dve.wait_ge(conv, n + 2)
                STT(out=TA[:, 2:S], in0=x[:, 0:S - 2], scalar=tap(1), in1=TA[:, 2:S], op0=ALU.mult, op1=ALU.add).then_inc(conv, 1)
                dve.wait_ge(conv, n + 3)
                V.tensor_copy(TB[:, 0:3], TA[:, 0:3])
                STT(out=TB[:, 3:S], in0=x[:, 0:S - 3], scalar=tap(0), in1=TA[:, 3:S], op0=ALU.mult, op1=ALU.add).then_inc(
                    sem("conv_sum"), 1)
            stage("xbc", conv_tile)
            dve.wait_ge(sem("dt_w_hi"), 1)
            TT(WDL[:], WDR[:], WDH[:].bitcast(F32), ALU.subtract).then_inc(sem("dt_w_lo"), 1)
            dve.wait_ge(sem("dt_psum"), 1)
            TT(DTX[:], PS[0][:, 0:SC * SSD_HEADS].rearrange("p (c h) -> p c h", c=SC),
               par("dt_b", 0, SSD_HEADS).unsqueeze(1).broadcast_to([P, SC, SSD_HEADS]), ALU.add).then_inc(sem("dt_in"), 1)
            dve.wait_ge(sem("dt_log"), 3)
            chain.link(STT(out=DT[:], in0=DTX[:], scalar=0.0, in1=DTL[:], op0=ALU.max, op1=ALU.add))
            dve.wait_ge(sem("a_exp"), 1)
            STT(out=ADT[:], in0=DT[:], scalar=-1.0, in1=EAL[:].unsqueeze(1).broadcast_to([P, SC, SSD_HEADS]),
                op0=ALU.mult, op1=ALU.mult).then_inc(sem("adt"), 1)
            for g in range(2):
                dve.wait_ge(sem("ssd_cb_psum"), g + 1)
                V.tensor_copy(CBM[:, g], PS[(5, 0)[g]][:].rearrange("p (c t) -> p c t", c=SC)).then_inc(sem("ssd_cb"), 1)
            dve.wait_ge(sem("dt_decays"), 1)
            dve.wait_ge(sem("adt"), 1)
            for g in range(2):
                dve.wait_ge(sem("ssd_cb_masked"), g + 1)
                with dve.Fori(0, 4) as p:
                    chain.enter(p, 7)
                    n = p + 4 * g
                    heads = bass.ds(p * 2 + 8 * g, 2)

                    def by_head(t, c0, c1, width):
                        return t[:, c0:c1, heads].unsqueeze(3).broadcast_to([P, c1 - c0, 2, width])
                    V.tensor_copy(XST, row(XBC, n)).then_inc(sem("ssd_staged"), 1)
                    for c in range(SC):
                        TT(LSG[:, c], const("later").unsqueeze(1).broadcast_to([P, 2, P]),
                           ADT[:, c, heads].unsqueeze(2).broadcast_to([P, 2, P]), ALU.mult)
                    V.tensor_copy(ARP[:].rearrange("p c (h d) -> p c h d", h=2), by_head(ADT, 0, SC, SSD_P)).then_inc(
                        sem("ssd_lhs"), 1)
                    dve.wait_ge(sem("ssd_x_turned"), n + 1)
                    chain.link(TT(X1[:], PS[0][:].rearrange("p (c h d) -> p c h d", c=SC, h=2),
                                  by_head(DT, 0, SC, SSD_P), ALU.mult))
                    TT(X2[:], X1[:], by_head(DEND, 0, SC, SSD_P), ALU.mult).then_inc(sem("ssd_x12"), 1)
                    for hh in range(2):
                        dve.wait_ge(sem("ssd_seg_exp"), n * 2 + hh + 1)
                        TT(LM[:, hh], LM[:, hh], CBM[:, g], ALU.mult).then_inc(sem("ssd_m"), 1)
                    dve.wait_ge(sem("ssd_new"), n + 1)
                    chain.link(V.tensor_copy(STT_[:, 0, :], PS[4][:, 0:P]))
                    for c in (1, 2):
                        chain.link(TT(STT_[:, c, :].rearrange("p (h d) -> p h d", h=2),
                                      STT_[:, c - 1, :].rearrange("p (h d) -> p h d", h=2),
                                      CDEC[:, c, heads].unsqueeze(2).broadcast_to([P, 2, SSD_P]), ALU.mult))
                        ins = TT(STT_[:, c, :], STT_[:, c, :], PS[4][:, c * P:(c + 1) * P], ALU.add)
                        if c == 1:
                            chain.link(ins)
                        else:
                            ins.then_inc(sem("ssd_states"), 1)
                    dve.wait_ge(sem("ssd_y"), n + 1)
                    d_at = PCOL["d_skip"][0] + 4 * g
                    d_col, x = PA[:, bass.ds(p + d_at, 1)], row(XBC, n)
                    STT(out=x[:, 0:P], in0=x[:, 0:P], scalar=d_col, in1=PS[5][:, 0:P], op0=ALU.mult, op1=ALU.add)
                    chain.link(STT(out=TA[:, P:S], in0=x[:, P:S], scalar=d_col, in1=PS[5][:, P:S], op0=ALU.mult,
                                   op1=ALU.add))
                    dve.wait_ge(sem("ssd_row_exp"), n + 1)
                    chain.link(TT(TB[:, P:S], ERW[:, P:S], PS[0][:, P:S], ALU.mult))
                    TT(row(XBC, n)[:, P:S], TA[:, P:S], TB[:, P:S], ALU.add).then_inc(sem("ssd_done"), 1)
                    chain.leave(4)
            dve.wait_ge(sem("ssd_done"), 8)

            def z_tile(t, i, m):
                r = row(XBC, i * m + t)
                TT(r, r, ev("z_ssd", t), ALU.mult).then_inc(sem("ssd_gated"), 1)
            stage("z_ssd", z_tile)
            for g in range(2):
                rstd(f"ssd{g}")
                apply_norm("norm_ssd", lambda k: XBC[:, k, :], "g_ssd", lambda k: YSH[:, k, :],
                           lambda k: YSL[:, k, :], ks=range(4 * g, 4 * g + 4))
            branch("out2")
            boundary(2, "post_mix", "g_mix_post", 1.0)
            norm("xa", "norm_xa", "g_xa_pre")

            stage("xa_q")
            rstd("mem", MEM)
            apply_norm("norm_mem", lambda k: MR[:, k, :], "g_mem", lambda k: MH[:, k, :], lambda k: ML[:, k, :], MEM)
            stage("xa_kv")
            dve.wait_ge(s_acc, TILE0["xa_o"])
            with dve.Fori(0, XA_HEADS) as h:
                chain.enter(h, 2)
                V.tensor_copy(CQS[:], XQ[:, bass.ds(h * 2, 2), :])
                V.tensor_copy(CKS[:], XKV[:, bass.ds(h * 2, 2), :])
                V.tensor_copy(CVS[:], XKV[:, bass.ds(h * 2 + 8, 2), :]).then_inc(sem("xa_staged"), 1)
                dve.wait_ge(sem("xa_v_turned"), h + 1)
                V.tensor_copy(CVT[:], PS[0][:].rearrange("p (c f) -> p c f", c=2)).then_inc(sem("xa_v_tokens"), 1)
                dve.wait_ge(sem("xa_scored"), h + 1)
                for a in range(2):
                    ins = V.reduce_max(CMX[:, 2 * a:2 * a + 2], PS[1 + a][:].rearrange("p (i m) -> p i m", i=2), AX)
                chain.link(ins)
                TS(CNM[:], CMX[:], -(XA_DH ** -0.5), None, ALU.mult).then_inc(sem("xa_max"), 1)
                dve.wait_ge(sem("xa_exp"), h * SC + SC)
                chain.link(V.reciprocal(CSR[:], CSU[:]))
                TT(CP[:], CP[:], CSR[:].unsqueeze(2).broadcast_to([P, SC, MEM]), ALU.mult).then_inc(sem("xa_scaled"), 1)
                for e in range(2):
                    dve.wait_ge(sem("xa_pv"), h * 2 + e + 1)
                    free_product(PROD0["xa"] + e, h * 2)
                    V.tensor_copy(PR[:, (PROD0["xa"] + e) % 2, :], PS[(5, 0)[e]][:]).then_inc(s_pr, 1)
                for e in range(2):
                    low(PROD0["xa"] + e, h * 2, row(XOH, h * 2 + e), row(XOL, h * 2 + e))
                chain.leave(XA_HEADS)
            branch("xa_o")
            boundary(3, "post_xa", "g_xa_post", 1.0)
            norm("ffn2", "norm_ffn2", "g_ffn2_pre")
            ffn(2)
            boundary(4, "post_ffn2", "g_ffn2_post", 0.5)

        @block.tensor
        def _(pe):
            MM, TR = nc.tensor.matmul, nc.tensor.transpose

            def gemm(name, s, i, g, hi, lo, k0=0, n=S):
                c, nb, per = SLOT0[name] + s, WIDTH[SLOT0[name] + s], PER_TILE.get(name, 1)
                first, last = s % per == 0, s % per == per - 1
                tile = TILE0[name] + s // per
                pe.wait_ge(s_lo, i * g + c + 1)
                if first and tile >= 2:
                    pe.wait_ge(s_acc, i * (g // per) + tile - 1)
                parts = ((WH, hi), (WH, lo), (WL, hi))
                for r, (w, a) in enumerate(parts):
                    for k in range(nb):
                        ins = MM(ACC[tile % 2][:, 0:n], w[:, c % HL_RING, k * P:(k + 1) * P], a[:, k0 + k, 0:n],
                                 start=first and r == 0 and k == 0, stop=last and r == 2 and k == nb - 1)
                ins.then_inc(s_used, 1)

            def stage(name, hi, lo, products, n=S):
                pe.wait_ge(s_pl, products)
                run_stage(pe, name, lambda s, i, g: gemm(name, s, i, g, hi, lo, 0, n))

            def total(name, n=S, ks=None):
                q0, count = SUM_SQ0[name], SUMS[SUM_N[name]][1]
                for k in range(count):
                    pe.wait_ge(s_sq, q0 + k + 1)
                    MM(PS[5][:, 0:n], ones, SQ[:, (q0 + k) % 2, 0:n], start=k == 0, stop=k == count - 1).then_inc(s_squsd, 1)

            def branch_total(b):
                pe.wait_ge(s_fsq, EV_RING + (b + 1) * DK)
                MM(PS[5][:], ones, SSQ[:], start=True, stop=True).then_inc(s_psum, 1)

            def done(name):
                return PROD0[name] + dict(PRODUCTS)[name]

            def token_major(bank, w_hi, w_lo, cols):
                for c in range(SC):
                    for r, (a, w) in enumerate(((HH, w_hi), (HH, w_lo), (HL, w_hi))):
                        for k in range(DK):
                            ins = MM(PS[bank][:, c * cols:(c + 1) * cols], a[:, k, c * P:(c + 1) * P], w[:, k, :],
                                     start=r == 0 and k == 0, stop=r == 2 and k == DK - 1)
                return ins

            def turn(bank, src, blocks, to=0):
                for c in range(blocks):
                    ins = TR(PS[bank][:, to + c * P:to + (c + 1) * P], src[:, c * P:(c + 1) * P], ident)
                return ins

            pe.wait_ge(s_in, 64)
            total("pre")

            pe.wait_ge(s_pl, done("norm_pre"))

            def half_turn(t):
                pe.wait_ge(s_acc, TILE0["nsa_rope"] + t + 1)
                if t >= 2:
                    pe.wait_ge(sem("nsa_roped"), t - 1)
                MM(PS[t % 2][:], const("nsa_rot"), EV[:, (EV0["nsa_rope"] + t) % EV_RING, :], start=True,
                   stop=True).then_inc(sem("nsa_turned_half"), 1)
            for s in range(COUNT["nsa_rope"]):
                gemm("nsa_rope", s, 0, 4, HH, HL)
                if s:
                    half_turn(s - 1)
            gemm("nsa_plain", 0, 0, 4, HH, HL)
            half_turn(COUNT["nsa_rope"] - 1)
            for s in range(1, COUNT["nsa_plain"]):
                gemm("nsa_plain", s, 0, 4, HH, HL)
            pe.wait_ge(sem("gate_w_lo"), 1)
            token_major(2, WGH, WGL, 24).then_inc(sem("gate_psum"), 1)
            for n in range(2):
                pe.wait_ge(s_acc, TILE0["nsa_plain"] + n + 2)
                turn(3 + n, VN[:, 1 + n, :], SC).then_inc(sem("nsa_v_turned"), 1)

            pe.wait_ge(s_late["cmp_w"], 64)
            pe.wait_ge(sem("nsa_roped"), COUNT["nsa_rope"])
            for n, t in enumerate(("k", "v")):
                pe.wait_ge(sem("cmp_blocks"), n + 1)
                for j in range(2):
                    for b in range(16):
                        ins = MM(PS[n][:, j * 2 * N_CMP:(j + 1) * 2 * N_CMP], W1[t][:, b, j * P:(j + 1) * P],
                                 BLK[t][:, b, :], start=b == 0, stop=b == 15)
                ins.then_inc(sem("cmp_hidden"), 1)
            pe.wait_ge(sem("gate_sum"), 1)
            pe.wait_ge(sem("cmp_gelu"), 2)
            for g in range(2):
                for j in range(2):
                    MM(PS[2][DH * g:DH * (g + 1), 0:N_CMP], W2["k"][:, j, :], HG["k"][:, j, g * N_CMP:(g + 1) * N_CMP],
                       start=j == 0, stop=j == 1)
            for g in range(2):
                for j in range(2):
                    ins = MM(PS[2][0:N_CMP, P + DH * g:P + DH * (g + 1)], HG["v"][:, j, g * N_CMP:(g + 1) * N_CMP],
                             W2["v"][:, j, :], start=j == 0, stop=j == 1)
            ins.then_inc(sem("cmp_done"), 1)

            pe.wait_ge(sem("nsa_v_tokens"), 2)
            pe.wait_ge(sem("cmp_kv"), 1)
            pe.wait_ge(sem("gate_ready"), 1)

            def wide_scores(u):
                i, hh = divmod(u, 2)
                kw, rows = (i + 1) * P, slice(DH * hh, DH * (hh + 1))
                for b in range(2):
                    MM(PS[b][:, 0:kw], QST[rows, i * P:(i + 1) * P], QK[rows, 5 + b, 0:kw], start=True, stop=False)
                    MM(PS[b][:, i * P:kw], ident, const("causal"), start=False, stop=True)

            def cmp_scores(u):
                i, hh = divmod(u, 2)
                rows = slice(DH * hh, DH * (hh + 1))
                MM(PS[2][:, 0:N_CMP], QST[rows, i * P:(i + 1) * P], KCT[rows, 0:N_CMP], start=True, stop=False)
                MM(PS[2][:, 0:N_CMP], ident, const("cmp_mask")[:, i * 32:i * 32 + N_CMP], start=False,
                   stop=True).then_inc(sem("nsa_scored"), 1)

            with pe.Fori(0, NSA_PAIRS) as p:
                pe.wait_ge(sem("nsa_staged"), p + 1)
                wide_scores(0)
                cmp_scores(0)
                for u in range(8):
                    i, hh = divmod(u, 2)
                    rows, cols = slice(DH * hh, DH * (hh + 1)), slice(i * P, (i + 1) * P)
                    pe.wait_ge(sem("nsa_scaled"), p * 8 + u + 1)
                    turn(3, PB[:, 0:S], i + 1)
                    turn(4, PB[:, S:2 * S], i + 1)
                    TR(PS[2][0:N_CMP, P:2 * P], PB[:, 2 * S:2 * S + N_CMP], ident).then_inc(sem("nsa_turned"), 1)
                    if u < 7:
                        wide_scores(u + 1)
                    pe.wait_ge(sem("nsa_win_t"), p * 8 + u + 1)
                    if u < 7:
                        cmp_scores(u + 1)
                    pe.wait_ge(sem("nsa_sel_t"), p * 8 + u + 1)
                    for c in range(i + 1):
                        MM(PS[5][rows, cols], VS[:, c, rows], PTS[:, c, :], start=c == 0, stop=False)
                    for c in range(i + 1):
                        MM(PS[5][rows, cols], VW[:, c, rows], PTW[:, c, :], start=False, stop=False)
                    MM(PS[5][rows, cols], VCT[0:N_CMP, hh, :], PTC[0:N_CMP, :], start=False, stop=True).then_inc(
                        sem("nsa_pv"), 1)
            stage("z_nsa", HH, HL, done("norm_pre"))

            stage("ret_rope", HH, HL, done("norm_pre"))
            stage("ret_v", HH, HL, done("norm_pre"))
            with pe.Fori(0, RET_HEADS) as h:
                pe.wait_ge(sem("ret_v_staged"), h + 1)
                pe.wait_ge(sem("ret_staged"), h + 1)
                for e in range(2):
                    turn(e, EV[:, e, :], SC).then_inc(sem("ret_v_turned"), 1)
                for j in range(SC):
                    if j >= 2:
                        pe.wait_ge(sem("ret_decayed"), h * SC + j - 1)
                    MM(PS[(2, 5)[j % 2]][:, 0:S - j * P], RKS[:, j * P:(j + 1) * P], RQS[:, j * P:S], start=True,
                       stop=True).then_inc(sem("ret_scored"), 1)
                pe.wait_ge(sem("ret_v_tokens"), h * 2 + 2)
                for j in range(SC):
                    pe.wait_ge(sem("ret_decayed"), h * SC + j + 1)
                    for e in range(2):
                        ins = MM(PS[3 + e][:, j * P:S], RVT[:, j, e * P:(e + 1) * P], RSM[:, j, 0:S - j * P],
                                 start=j == 0, stop=j == SC - 1)
                ins.then_inc(sem("ret_pv"), 1)
                pe.wait_ge(sem("ret_raw"), h * 2 + 2)
                for e in range(2):
                    ins = MM(PS[0][:], ones_ret, row(ORT, h * 2 + e), start=e == 0, stop=e == 1)
                ins.then_inc(sem("ret_mean"), 1)
                pe.wait_ge(sem("ret_sq"), h * 2 + 2)
                for e in range(2):
                    ins = MM(PS[1][:], ones_ret, EV[:, 2 + e, :], start=e == 0, stop=e == 1)
                ins.then_inc(sem("ret_var"), 1)
            stage("z_ret", HH, HL, done("z_nsa"))

            pe.wait_ge(s_pl, done("z_ret"))

            def merge_slot(s, i, g):
                hi, lo = ((HH, HL), (GAH, GAL), (HH, HL), (GRH, GRL))[s % 4]
                gemm("merge", s, i, g, hi, lo)
            run_stage(pe, "merge", merge_slot)
            stage("out1", MGH, MGL, done("merge"))
            branch_total(0)
            total("ffn1")

            def ffn(n):
                stage(f"ffn{n}_up", HH, HL, done(f"norm_ffn{n}"))
                pe.wait_ge(s_pl, done(f"ffn{n}"))
                run_stage(pe, f"ffn{n}_down", lambda s, i, g: gemm(f"ffn{n}_down", s, i, g, AH, AL, (s % 2) * HALF_FK))
            ffn(1)
            branch_total(1)
            total("mix")

            stage("sb_qkv", HH, HL, done("norm_mix"))
            tri, neg = const("neg_incl"), const("neg_ones")

            def place_of(hh, j):
                return ((hh, 0), (2 + hh, 0), (4, 2 * P * hh), (2 + hh, 3 * P))[j]

            with pe.Fori(0, SB_PAIRS) as p:
                pe.wait_ge(sem("sb_staged"), p + 1)
                turn(5, BVS, SC).then_inc(sem("sb_v_turned"), 1)
                def scores(hh, j):
                    b, at = place_of(hh, j)
                    rows = slice(DH * hh, DH * (hh + 1))
                    return MM(PS[b][:, at:at + S - j * P], BKS[rows, j * P:(j + 1) * P], BQS[rows, j * P:S],
                              start=at == 0, stop=True, skip_group_check=True)
                scores(0, 2).then_inc(sem("sb_first_half"), 1)
                for b in range(4):
                    ins = scores(b % 2, b // 2)
                    if b >= 2:
                        ins = scores(b % 2, 3)
                    ins.then_inc(sem("sb_scored"), 1)
                pe.wait_ge(sem("sb_first_half"), p + 1)
                scores(1, 2).then_inc(sem("sb_scored"), 1)
                pe.wait_ge(sem("sb_softplus_masked"), p * 5 + 5)
                for b in range(5):
                    for hh, j in ([(0, 0)], [(1, 0)], [(0, 1), (0, 3)], [(1, 1), (1, 3)], [(0, 2), (1, 2)])[b]:
                        at, end = place_of(hh, j)[1], place_of(hh, j)[1] + S - j * P
                        for later in range(j, SC):
                            sb_, sat = place_of(hh, later)
                            n = S - later * P
                            ins = MM(PS[b][:, end - n:end], tri if later == j else neg, SPB[:, sb_, sat:sat + n],
                                     start=False, stop=True, skip_group_check=True)
                    ins.then_inc(sem("sb_suffixed"), 1)
                pe.wait_ge(sem("sb_exp_masked"), p * 5 + 5)
                for hh in range(2):
                    rows = slice(DH * hh, DH * (hh + 1))
                    for j in range(SC):
                        b, at = place_of(hh, j)
                        ins = MM(PS[5][rows, j * P:S], BVT[:, j, rows], sb_tmp(b)[:, at:at + S - j * P], start=j == 0,
                                 stop=j == SC - 1)
                ins.then_inc(sem("sb_pv"), 1)
            total("attn")

            stage("xbc", HH, HL, done("norm_mix"))
            pe.wait_ge(sem("dt_w_lo"), 1)
            token_major(0, WDH, WDL, SSD_HEADS).then_inc(sem("dt_psum"), 1)
            pe.wait_ge(sem("conv_silu"), 1 + CONV_TILES)
            for g in range(2):
                turn(3 + g, XBC[:, 8 + g, :], SC).then_inc(sem("ssd_bt"), 1)
            pe.wait_ge(sem("adt"), 1)
            MM(PS[1][:, 0:64], const("later"), ADT[:].rearrange("p c h -> p (c h)"), start=True, stop=True)
            MM(PS[2][:, 0:64], ones, ADT[:].rearrange("p c h -> p (c h)"), start=True, stop=True).then_inc(sem("dt_sums"), 1)
            for g in range(2):
                for c in range(SC):
                    cols = slice(c * P, (c + 1) * P)
                    ins = MM(PS[(5, 0)[g]][:, cols], XBC[:, 8 + g, cols], XBC[:, 10 + g, cols], start=True, stop=True)
                ins.then_inc(sem("ssd_cb_psum"), 1)
            pe.wait_ge(sem("ssd_b_tokens"), 2)
            pe.wait_ge(sem("dt_decays"), 1)
            for g in range(2):
                with pe.Fori(0, 4) as p:
                    n = p + 4 * g
                    pe.wait_ge(sem("ssd_staged"), n + 1)
                    turn(0, XST, SC).then_inc(sem("ssd_x_turned"), 1)
                    pe.wait_ge(sem("ssd_lhs"), n + 1)
                    for hh in range(2):
                        for c in range(SC):
                            ins = MM(PS[1 + hh][:, c * P:(c + 1) * P], LSG[:, c, hh, :], const("upper_incl"), start=True,
                                     stop=True)
                    ins.then_inc(sem("ssd_seg"), 1)
                    for c in range(1, SC):
                        ins = MM(PS[3][:, c * P:(c + 1) * P], ARP[:, c, :], const("upper_incl"), start=True, stop=True)
                    ins.then_inc(sem("ssd_rows"), 1)
                    pe.wait_ge(sem("ssd_x12"), n + 1)
                    for c in range(SC - 1):
                        ins = MM(PS[4][:, c * P:(c + 1) * P], BTK[:, g, c, :], X2[:, c].rearrange("p h d -> p (h d)"),
                                 start=True, stop=True)
                    ins.then_inc(sem("ssd_new"), 1)
                    pe.wait_ge(sem("ssd_m"), n * 2 + 2)
                    for hh in range(2):
                        for c in range(SC):
                            MM(PS[5][DH * hh:DH * (hh + 1), c * P:(c + 1) * P], X1[:, c, hh, :], LM[:, hh, c, :],
                               start=True, stop=True)
                    pe.wait_ge(sem("ssd_states"), n + 1)
                    for c in range(1, SC):
                        ins = MM(PS[0][:, c * P:(c + 1) * P], STT_[:, c - 1, :], XBC[:, 10 + g, c * P:(c + 1) * P],
                                 start=True, stop=True)
                    ins.then_inc(sem("ssd_y"), 1)
            stage("z_ssd", HH, HL, done("norm_mix"))
            total("ssd0")
            total("ssd1")
            pe.wait_ge(s_pl, done("norm_ssd"))
            run_stage(pe, "out2", lambda s, i, g: gemm("out2", s, i, g, *((OSH, OSL), (YSH, YSL))[s % 2]))
            branch_total(2)
            total("xa")

            stage("xa_q", HH, HL, done("norm_xa"))
            total("mem", MEM)
            stage("xa_kv", MH, ML, done("norm_mem"), MEM)
            with pe.Fori(0, XA_HEADS) as h:
                pe.wait_ge(sem("xa_staged"), h + 1)
                for mc in range(2):
                    for e in range(2):
                        ins = TR(PS[0][:, (mc * 2 + e) * P:(mc * 2 + e + 1) * P], CVS[:, e, mc * P:(mc + 1) * P], ident)
                ins.then_inc(sem("xa_v_turned"), 1)
                for i in range(SC):
                    for e in range(2):
                        ins = MM(PS[1 + i // 2][:, (i % 2) * MEM:(i % 2 + 1) * MEM], CQS[:, e, i * P:(i + 1) * P],
                                 CKS[:, e, :], start=e == 0, stop=e == 1)
                ins.then_inc(sem("xa_scored"), 1)
                pe.wait_ge(sem("xa_scaled"), h + 1)
                for mc in range(2):
                    for i in range(SC):
                        ins = TR(PS[3 + mc][:, i * P:(i + 1) * P], CP[:, i, mc * P:(mc + 1) * P], ident)
                    ins.then_inc(sem("xa_turned"), 1)
                pe.wait_ge(sem("xa_v_tokens"), h + 1)
                pe.wait_ge(sem("xa_probs_t"), h * 2 + 2)
                for e in range(2):
                    for mc in range(2):
                        ins = MM(PS[(5, 0)[e]][:], CVT[:, mc, e * P:(e + 1) * P], CPT[:, mc, :], start=mc == 0,
                                 stop=mc == 1)
                    ins.then_inc(sem("xa_pv"), 1)
            stage("xa_o", XOH, XOL, done("xa"))
            branch_total(3)
            total("ffn2")
            ffn(2)
            branch_total(4)


def shape_constants():
    k, m = np.arange(P)[:, None], np.arange(P)[None, :]
    rot = np.zeros((P, P))
    for d in range(P):
        if d % DH < 8:
            rot[d + 8, d] = 1
        elif d % DH < 16:
            rot[d - 8, d] = 1
    q = np.arange(S).reshape(SC, P).T[:, :, None]
    seen = (np.arange(32)[None, None, :] * CMP_STRIDE + CMP_LEN - 1 <= q)
    parts = {"ident": np.eye(P), "ones": np.ones((P, P)), "ones_ret": np.full((P, P), 1.0 / RET_DV), "nsa_rot": rot,
             "causal": np.where(m > k, NEG, 0.0), "neg_incl": -1.0 * (k >= m), "neg_ones": -np.ones((P, P)),
             "upper_incl": 1.0 * (k <= m), "later": 1.0 * (k > m),
             "cmp_mask": np.where(seen, 0.0, NEG).reshape(P, -1), "cmp_keep": (1.0 * seen).reshape(P, -1)}
    consts = np.concatenate([parts[n] for n, _ in CONSTS], axis=1).astype(np.float32)

    pos = np.arange(S, dtype=np.float32)
    rope = np.zeros((P, 4, S), np.float32)
    rope[:, 0] = 1.0
    inv = (1.0 / (500000.0 ** (np.arange(0, 16, 2, dtype=np.float32) / 16))).astype(np.float32)
    for d in range(P):
        if d % DH < 16:
            ang = pos * inv[d % 8]
            rope[d, 0] = np.cos(ang)
            rope[d, 1] = np.sin(ang) * (-1 if d % DH < 8 else 1)
    inv = (1.0 / (10000.0 ** np.linspace(0.0, 1.0, RET_DK // 2, dtype=np.float32))).astype(np.float32)
    ang = pos[None, :] * inv[np.arange(P) % 64][:, None]
    rope[:, 2] = np.cos(ang)
    rope[:, 3] = np.sin(ang) * np.where(np.arange(P) < 64, 1, -1)[:, None]

    dist = np.arange(S)[None, :] - np.arange(P)[:, None]
    log_g = np.log(1.0 - 2.0 ** (-5.0 - np.arange(RET_HEADS)))
    decay = np.where(dist[:, None, :] >= 0, np.exp(np.maximum(dist, 0)[:, None, :] * log_g[None, :, None]), 0.0)
    decay = (decay * RET_DK ** -0.5).astype(np.float32)
    return consts, rope, decay


def tiles(w):
    kk, mm = w.shape
    return w.reshape(kk // P, P, mm // P, P).transpose(1, 2, 0, 3)


def flat(w):
    return w.reshape(P, -1)


def columns(v):
    return v.reshape(-1, P).T


def stream(w_in, w_nsa_o, w_ret_o, w_out, ffn, w_in2, w_out2, wq, wkv, wo, pairs):
    at = np.cumsum([0, 512, 128, 128, 128, 128, 128, 128, 24, 512, 512, 512, 1024, 1024, D, D])
    (q_n, k_c, v_c, k_s, v_s, k_w, v_w, _, z_n, q_r, k_r, v_r, z_r, m_a, m_b) = [
        w_in[:, a:b] for a, b in zip(at[:-1], at[1:])]
    out = [flat(tiles(w)) for w in (q_n[:, pairs], k_c, k_s, k_w, v_c, v_s, v_w, z_n[:, pairs], q_r, k_r, v_r, z_r)]
    ma, mb, ya, yb = tiles(m_a), tiles(m_b), tiles(w_nsa_o[pairs]), tiles(w_ret_o)
    for m in range(DK):
        out += [flat(ma[:, m]), flat(ya[:, m]), flat(mb[:, m]), flat(yb[:, m])]
    out.append(flat(tiles(w_out)))

    def feed_forward(gu, down):
        g, u = tiles(gu[:, :FF]), tiles(gu[:, FF:])
        return [flat(np.stack([g, u], axis=2)), flat(tiles(down))]
    out += feed_forward(*ffn[0])
    q, k, v, z, xbc, _ = np.split(w_in2, [1024, 2048, 3072, 4096, 4096 + CONV_TILES * P], axis=1)
    out += [flat(tiles(w)) for w in (q, k, v, xbc, z, w_out2, wq, wkv, wo)]
    out += feed_forward(*ffn[1])
    return np.concatenate(out, axis=1)


def narrow(w):
    return w.reshape(DK, P, -1).transpose(1, 0, 2)


def kernel(x, norm_pre, w_in, b_nsa_gate, cmp_pe_k, cmp_w1_k, cmp_w2_k, cmp_pe_v, cmp_w1_v, cmp_w2_v, w_nsa_o,
           w_ret_o, w_out, norm_post, mem_2, ffn1_pre_g_2, ffn1_w_gu_2, ffn1_w_down_2, ffn1_post_g_2, mix_pre_g_2,
           w_in_2, conv_w_2, conv_b_2, dt_bias_2, a_log_2, d_skip_2, ssd_norm_g_2, attn_norm_g_2, w_out_2,
           mix_post_g_2, xa_pre_g_2, mem_g_2, xa_wq_2, xa_wkv_2, xa_wo_2, xa_post_g_2, ffn2_pre_g_2, ffn2_w_gu_2,
           ffn2_w_down_2, ffn2_post_g_2):
    import concourse.bacc as bacc
    from concourse.bass_utils import run_bass_kernel_spmd

    a = {n: np.asarray(v) for n, v in locals().items() if hasattr(v, "shape")}

    pairs = np.concatenate([np.arange(DH) + DH * h for p in range(NSA_PAIRS) for h in (p, p + NSA_PAIRS)])

    def spread(v):
        return np.broadcast_to(v.reshape(1, -1), (P, v.size))

    def positions(pe):
        v = pe.reshape(16, 2, DH).transpose(2, 1, 0).reshape(DH, 32)
        return np.concatenate([v, v], axis=0)

    def hidden(w1):
        return w1.reshape(16, 2, DH, CMP_HIDDEN).transpose(1, 2, 0, 3).reshape(P, 16, CMP_HIDDEN)

    conv_w = a["conv_w_2"][0]
    values = {
        "g_pre": columns(a["norm_pre"]), "g_post": columns(a["norm_post"]),
        "g_ffn1_pre": columns(a["ffn1_pre_g_2"][0]), "g_ffn1_post": columns(a["ffn1_post_g_2"][0]),
        "g_mix_pre": columns(a["mix_pre_g_2"][0]), "g_attn": columns(a["attn_norm_g_2"][0]),
        "g_ssd": columns(a["ssd_norm_g_2"][0]), "g_mix_post": columns(a["mix_post_g_2"][0]),
        "g_xa_pre": columns(a["xa_pre_g_2"][0]), "g_mem": columns(a["mem_g_2"][0]),
        "g_xa_post": columns(a["xa_post_g_2"][0]), "g_ffn2_pre": columns(a["ffn2_pre_g_2"][0]),
        "g_ffn2_post": columns(a["ffn2_post_g_2"][0]), "conv_b": columns(a["conv_b_2"][0]),
        "conv_w": np.concatenate([columns(conv_w[k]) for k in range(CONV_K)], axis=1),
        "d_skip": columns(np.repeat(a["d_skip_2"][0], SSD_P)), "gate_b": spread(a["b_nsa_gate"]),
        "dt_b": spread(a["dt_bias_2"][0]), "a_log": spread(a["a_log_2"][0]),
        "pe_k": positions(a["cmp_pe_k"]), "pe_v": positions(a["cmp_pe_v"]),
    }
    consts, rope, decay = shape_constants()
    w2in = a["w_in_2"][0]
    data = {
        "xT": a["x"][0].T.reshape(DK, P, S).transpose(1, 0, 2),
        "mem_t": a["mem_2"][0].T.reshape(DK, P, MEM).transpose(1, 0, 2),
        "w_all": stream(a["w_in"], a["w_nsa_o"], a["w_ret_o"], a["w_out"],
                        [(a["ffn1_w_gu_2"][0], a["ffn1_w_down_2"][0]), (a["ffn2_w_gu_2"][0], a["ffn2_w_down_2"][0])],
                        w2in, a["w_out_2"][0], a["xa_wq_2"][0], a["xa_wkv_2"][0], a["xa_wo_2"][0], pairs),
        "params": np.concatenate([values[n] for n, _ in PARAMS], axis=1),
        "consts": consts, "rope": rope, "decay": decay,
        "w_gate": narrow(a["w_in"][:, 1280:1304]), "w_dt": narrow(w2in[:, -SSD_HEADS:]),
        "w1k": hidden(a["cmp_w1_k"]), "w1v": hidden(a["cmp_w1_v"]),
        "w2k": a["cmp_w2_k"].reshape(2, P, DH).transpose(1, 0, 2),
        "w2v": a["cmp_w2_v"].reshape(2, P, DH).transpose(1, 0, 2),
    }
    nc = bacc.Bacc("TRN2", target_bir_lowering=False, num_devices=1)
    arrays, args = {}, []
    for name, v in data.items():
        v = np.ascontiguousarray(v)
        arrays[name] = v
        args.append(nc.dram_tensor(name, v.shape, mybir.dt.from_np(v.dtype), kind="ExternalInput").ap())
    args.append(nc.dram_tensor("out_t", (P, DK, S), F32, kind="ExternalOutput").ap())
    block_program(nc, *args)
    r = run_bass_kernel_spmd(nc, [arrays], core_ids=[0])
    out = np.asarray(r.results[0]["out_t"])
    return np.ascontiguousarray(out.transpose(1, 0, 2).reshape(D, S).T).reshape(a["x"].shape)
```

```python
from contextlib import ExitStack

import numpy as np

import concourse.bass as bass
from concourse import mybir

F32 = mybir.dt.float32
F32R = mybir.dt.float32r
ACT = mybir.ActivationFunctionType
ALU = mybir.AluOpType
AX = mybir.AxisListType.X

P = 128
S = 512
SC = S // P
D = 1024
DK = D // P
FF = 2816
FK = FF // P
HALF_FK = FK // 2
EPS = 1e-6
NEG = -1e30
TINY = float(np.finfo(np.float32).tiny)

NSA_HEADS, NSA_GROUPS, DH = 8, 2, 64
NSA_PAIRS = NSA_HEADS // 2
NSA_SCALE = DH ** -0.5
CMP_LEN, CMP_STRIDE, CMP_HIDDEN = 32, 16, 256
N_CMP = (S - CMP_LEN) // CMP_STRIDE + 1
RET_HEADS, RET_DK, RET_DV = 4, 128, 256
SB_PAIRS = 8
SSD_HEADS, SSD_P, SSD_N = 16, 64, 128
CONV_K = 4
CONV_TILES = 12
CONV_ORDER = [8, 10, 9, 11, 0, 1, 2, 3, 4, 5, 6, 7]
MEM = 256
XA_HEADS, XA_DH = 4, 256

RAW_RING = 4
HL_RING = 2
EV_RING = 4

PARAMS = [("g_pre", DK), ("g_post", DK), ("g_ffn1_pre", DK), ("g_ffn1_post", DK), ("g_mix_pre", DK),
          ("g_attn", DK), ("g_ssd", DK), ("g_mix_post", DK), ("g_xa_pre", DK), ("g_mem", DK),
          ("g_xa_post", DK), ("g_ffn2_pre", DK), ("g_ffn2_post", DK), ("conv_b", CONV_TILES),
          ("conv_w", CONV_K * CONV_TILES), ("d_skip", DK), ("gate_b", 24), ("dt_b", SSD_HEADS),
          ("a_log", SSD_HEADS), ("pe_k", 32), ("pe_v", 32)]
PCOL = {}
_at = 0
for _n, _w in PARAMS:
    PCOL[_n] = (_at, _at + _w)
    _at += _w
NPARAM = _at

CONSTS = [("ident", P), ("ones", P), ("ones_ret", P), ("nsa_rot", P), ("causal", P), ("neg_incl", P),
          ("neg_ones", P), ("upper_incl", P), ("later", P), ("cmp_mask", SC * 32), ("cmp_keep", SC * 32)]
CCOL = {}
_at = 0
for _n, _w in CONSTS:
    CCOL[_n] = (_at, _at + _w)
    _at += _w
NCONST = _at

STAGES = [
    ("nsa_rope", 7, (8,), "ev"), ("nsa_plain", 3, (8,), "plain"), ("ret_in", 16, (8,), "held"),
    ("z_ret", 8, (8,), "held"), ("z_nsa", 4, (8,), "ev"),
    ("merge", 32, (8, 4, 8, 8), "ev"), ("out1", 8, (8,), "ev"),
    ("ffn1_up", 44, (8,), "ev"), ("ffn1_down", 16, (11,), "ev"),
    ("sb_qkv", 24, (8,), "plain"), ("ssd_early", 16, (8,), "held"), ("ssd_late", 4, (8,), "held"),
    ("out2", 16, (8,), "ev"), ("xa_q", 8, (8,), "plain"), ("xa_kv", 16, (8,), "plain"),
    ("xa_o", 8, (8,), "ev"), ("ffn2_up", 44, (8,), "ev"), ("ffn2_down", 16, (11,), "ev"),
]
PER_TILE = {"ffn1_down": 2, "ffn2_down": 2, "out2": 2}
SLOT0, TILE0, EV0, WIDTH, COL0 = {}, {}, {}, [], {}
_s = _t = _e = _c = 0
for _n, _k, _w, _how in STAGES:
    SLOT0[_n], TILE0[_n], EV0[_n], COL0[_n] = _s, _t, _e, _c
    WIDTH += [_w[j % len(_w)] for j in range(_k)]
    _c += sum(_w[j % len(_w)] for j in range(_k)) * P
    _s += _k
    _t += _k // PER_TILE.get(_n, 1)
    _e += _k // PER_TILE.get(_n, 1) if _how == "ev" else 0
N_SLOTS, W_COLS = _s, _c
COUNT = {n: k for n, k, _, _ in STAGES}

PRODUCTS = [("norm_pre", DK), ("gates", 12), ("merge", 8), ("norm_ffn1", DK), ("ffn1", FK),
            ("norm_mix", DK), ("norm_attn", DK), ("norm_ssd", DK), ("norm_xa", DK), ("norm_mem", DK),
            ("xa", 8), ("norm_ffn2", DK), ("ffn2", FK)]
PROD0 = {}
_at = 0
for _n, _w in PRODUCTS:
    PROD0[_n] = _at
    _at += _w

SUMS = [("pre", DK), ("post1", 1), ("ffn1", DK), ("post_ffn1", 1), ("mix", DK), ("attn", DK), ("ssd0", 4),
        ("ssd1", 4), ("post_mix", 1), ("xa", DK), ("mem", DK), ("post_xa", 1), ("ffn2", DK), ("post_ffn2", 1)]
SUM_N, SUM_SQ0 = {}, {}
_at = 0
for _j, (_n, _w) in enumerate(SUMS):
    SUM_N[_n], SUM_SQ0[_n] = _j, _at
    _at += _w if _w > 1 else 0


BRANCH = {"out1": 0, "ffn1_down": 1, "out2": 2, "xa_o": 3, "ffn2_down": 4}
POST = {"post1": 0, "post_ffn1": 1, "post_mix": 2, "post_xa": 3, "post_ffn2": 4}
GROUP = {"merge": 8}


def run_stage(eng, name, body):
    base, n, g = SLOT0[name], COUNT[name], GROUP.get(name, 4)
    same = base + n < N_SLOTS and WIDTH[base + n] == WIDTH[base] and n % g == 0
    loops = n // g - (0 if same else 1)
    done = 0
    if loops >= 2 and base >= RAW_RING:
        with eng.Fori(0, loops) as i:
            for s in range(g):
                body(s, i, g)
        done = loops * g
    for s in range(done, n):
        body(s, 0, g)


def wait_apart(eng, sem, value, seen):
    eng.wait_ge(sem, value)
    eng.sem_inc(seen, 1)


def row(tensor, k):
    return tensor[:, bass.ds(k, 1), :].rearrange("p a s -> p (a s)")


class Tally:

    def __init__(self, eng, sem):
        self.eng, self.sem, self.base, self.k, self.i, self.per = eng, sem, 0, 0, None, 0

    def enter(self, i, per):
        self.base += self.k
        self.k, self.i, self.per = 0, i, per

    def leave(self, trips):
        assert self.k == self.per, (self.k, self.per)
        self.base += trips * self.per
        self.k, self.i = 0, None

    def link(self, ins):
        ins.then_inc(self.sem, 1)
        self.k += 1
        value = self.base + self.k
        self.eng.wait_ge(self.sem, value if self.i is None else self.i * self.per + value)


def block_program(nc, xT, mem_t, w_all, params, consts, rope, decay, w_gate, w_dt, w1k, w1v, w2k, w2v, out_t):
    ctx = ExitStack()
    with ctx:
        sems = {}

        def sem(name):
            if name not in sems:
                sems[name] = ctx.enter_context(nc.semaphore(name))
            return sems[name]

        def sb(name, shape, dt=F32):
            return ctx.enter_context(nc.sbuf_tensor(name, shape, dt))

        X = sb("residual", [P, DK, S])
        SLOT = HALF_FK * P
        WR = sb("w_raw", [P, RAW_RING, SLOT])
        WH = sb("w_hi", [P, HL_RING, SLOT], F32R)
        WL = sb("w_lo", [P, HL_RING, SLOT], F32R)
        EV = sb("evacuated", [P, EV_RING, S])
        PR = sb("product", [P, 2, S])
        SSQ = sb("square_sum", [P, S])
        RM = sb("root_mean", [P, S])
        RS = sb("rstd", [P, S])
        PA = sb("param_cols", [P, NPARAM])
        CO = sb("const_cols", [P, NCONST])
        arena0 = nc.sbuf_base
        arena_end = nc.sbuf_usable_end

        def place(name, shape, off, dt=F32):
            size = int(np.prod(shape[1:])) * 4
            assert arena0 + off * 1024 + size <= arena_end, (name, off, size, (arena_end - arena0) / 1024)
            return nc.alloc_sbuf_tensor_at(name, shape, dt, offset=arena0 + int(off * 1024))

        def par(name, j=0, n=1):
            a = PCOL[name][0] + j
            return PA[:, a:a + n]

        def const(name):
            return CO[:, CCOL[name][0]:CCOL[name][1]]

        ACC = [ctx.enter_context(nc.psum_tensor(f"acc{b}", [P, S], F32)) for b in range(2)]
        PS = [ctx.enter_context(nc.psum_tensor(f"bank{b}", [P, S], F32)) for b in range(6)]

        HH = place("act_hi", [P, DK, S], 0, F32R)
        HL = place("act_lo", [P, DK, S], 16, F32R)
        FO = place("branch_out", [P, DK, S], 0)
        TA = place("tmp_a", [P, S], 115)
        TB = place("tmp_b", [P, S], 117)
        SQ = place("squares", [P, 2, S], 119)
        CR = SQ
        QK = place("nsa_qk", [P, 7, S], 32)
        VN = place("nsa_v", [P, 3, S], 46)
        ROPE_N = place("nsa_rope_table", [P, 2, S], 52)
        ROPE_R = place("ret_rope_table", [P, 2, S], 56)
        W1 = {"k": place("cmp_w1_k", [P, 16, CMP_HIDDEN], 60), "v": place("cmp_w1_v", [P, 16, CMP_HIDDEN], 76)}
        BLK = {"k": place("cmp_blocks_k", [P, 16, 2 * N_CMP], 92), "v": place("cmp_blocks_v", [P, 16, 2 * N_CMP], 96)}
        HG = {"k": place("cmp_hidden_k", [P, 2, 2 * N_CMP], 100), "v": place("cmp_hidden_v", [P, 2, 2 * N_CMP], 100.5)}
        W2 = {"k": place("cmp_w2_k", [P, 2, DH], 101), "v": place("cmp_w2_v", [P, 2, DH], 101.5)}
        KCT = place("cmp_keys", [P, 32], 112)
        VCT = place("cmp_values", [P, 2, DH], 112.25)
        VS = place("sel_values", [P, SC, P], 108)
        VW = place("win_values", [P, SC, P], 110)
        GT = place("nsa_gates", [P, SC, 24], 113)
        WGR = place("gate_w_raw", [P, DK, 24], 108)
        WGH = place("gate_w_hi", [P, DK, 24], 109, F32R)
        WGL = place("gate_w_lo", [P, DK, 24], 110, F32R)
        QST = place("nsa_q_stage", [P, S], 60)
        PB = place("nsa_probs", [P, 2 * S + 32], 62)
        PTS = place("sel_probs_t", [P, SC, P], 67)
        PTW = place("win_probs_t", [P, SC, P], 69)
        PTC = place("cmp_probs_t", [P, P], 71)
        MX = place("nsa_max", [P, 4], 72)
        NM = place("nsa_neg_max", [P, 4], 72.25)
        SU = place("nsa_sums", [P, 4], 72.5)
        SR = place("nsa_sum_recip", [P, 4], 72.75)
        SW = place("nsa_weights", [P, 4], 73)
        OA = place("nsa_out", [P, 4, S], 32)
        GAH = place("nsa_gated_hi", [P, 4, S], 106, F32R)
        GAL = place("nsa_gated_lo", [P, 4, S], 48, F32R)
        RQK = place("ret_qk", [P, 8, S], 74)
        RSM = place("ret_scores", [P, SC, S], 40)
        RQS = place("ret_q_stage", [P, S], 48)
        RKS = place("ret_k_stage", [P, S], 50)
        RVT = place("ret_v_tokens", [P, SC, RET_DV], 52)
        RDEC = place("ret_decay", [P, S], 72)
        RV = place("ret_v", [P, 8, S], 90)
        ORT = place("ret_out", [P, 8, S], 56)
        GRH = place("ret_gated_hi", [P, 8, S], 90, F32R)
        GRL = place("ret_gated_lo", [P, 8, S], 56, F32R)
        MGL = place("merged_lo", [P, 8, S], 32, F32R)
        MGH = place("merged_hi", [P, 8, S], 74, F32R)
        AH = place("ffn_hi", [P, FK, S], 32, F32R)
        AL = place("ffn_lo", [P, FK, S], 76, F32R)
        QKV = place("sb_qkv", [P, 24, S], 32)
        OSB = place("sb_out", [P, 8, S], 80)
        BQS = place("sb_q_stage", [P, S], 96)
        BKS = place("sb_k_stage", [P, S], 98)
        BVS = place("sb_v_stage", [P, S], 100)
        BVT = place("sb_v_tokens", [P, SC, P], 102)
        SPB = place("sb_softplus", [P, 5, S], 104)
        OSH = place("sb_hi", [P, 8, S], 32, F32R)
        OSL = place("sb_lo", [P, 8, S], 80, F32R)
        XB = place("ssd_xbc", [P, 8, S], 48)
        ZS = place("ssd_z", [P, 8, S], 64)
        XT = place("ssd_x_late", [P, 4, S], 96)
        BTK = place("ssd_b_tokens", [P, 2, SC, P], 0)
        CBM = place("ssd_cb", [P, 2, SC, P], 4)
        XST = EV[:, 1, :]
        NROWS = EV[:, 3, :]
        X1 = place("ssd_x_dt", [P, SC, 2, SSD_P], 8)
        X2 = place("ssd_x_decayed", [P, SC, 2, SSD_P], 10)
        LSG = place("ssd_segments", [P, SC, 2, P], 12)
        LM = place("ssd_decays", [P, 2, SC, P], 104)
        ARP = place("ssd_adt_rows", [P, SC, P], 108)
        ERW = EV[:, 0, :]
        STT_ = place("ssd_states", [P, 3, P], 110)
        WDR = place("dt_w_raw", [P, DK, SSD_HEADS], 111.5)
        WDH = place("dt_w_hi", [P, DK, SSD_HEADS], 112, F32R)
        WDL = place("dt_w_lo", [P, DK, SSD_HEADS], 112.5, F32R)
        DTX = place("dt_in", [P, SC, SSD_HEADS], 113.5)
        DTL = place("dt_log", [P, SC, SSD_HEADS], 113.75)
        DT = place("dt", [P, SC, SSD_HEADS], 114)
        ADT = place("a_dt", [P, SC, SSD_HEADS], 114.25)
        DEND = place("decay_to_end", [P, SC, SSD_HEADS], 114.5)
        CDEC = place("chunk_decay", [P, SC, SSD_HEADS], 114.75)
        EAL = place("a_exp", [P, SSD_HEADS], 113)
        YSH = place("ssd_hi", [P, 8, S], 64, F32R)
        YSL = place("ssd_lo", [P, 8, S], 16, F32R)
        XQ = place("xa_q", [P, 8, S], 32)
        XKV = place("xa_kv", [P, 16, MEM], 48)
        MR = place("mem_raw", [P, DK, MEM], 64)
        MH = place("mem_hi", [P, DK, MEM], 72, F32R)
        ML = place("mem_lo", [P, DK, MEM], 80, F32R)
        XOH = place("xa_hi", [P, 8, S], 72, F32R)
        XOL = place("xa_lo", [P, 8, S], 88, F32R)
        CQS = place("xa_q_stage", [P, 2, S], 64)
        CKS = place("xa_k_stage", [P, 2, MEM], 68)
        CVS = place("xa_v_stage", [P, 2, MEM], 70)
        CVT = place("xa_v_tokens", [P, 2, XA_DH], 104)
        CP = place("xa_probs", [P, SC, MEM], 106)
        CPT = place("xa_probs_t", [P, 2, S], 110)
        CMX = place("xa_max", [P, SC], 114)
        CNM = place("xa_neg_max", [P, SC], 114.25)
        CSU = place("xa_sums", [P, SC], 114.5)
        CSR = place("xa_sum_recip", [P, SC], 114.75)

        ident, ones, ones_ret = const("ident"), const("ones"), const("ones_ret")
        s_in = sem("inputs_landed")
        s_xin = sem("x_landed")
        s_late = {n: sem(n + "_landed") for n in ("cmp_w", "rope_ret", "decay", "mem", "dt_w")}
        s_raw = [sem(f"w_landed{r}") for r in range(RAW_RING)]
        s_hi, s_lo, s_used = sem("w_hi_ready"), sem("w_lo_ready"), sem("w_slot_used")
        s_acc = sem("acc_evacuated")
        s_sq, s_squsd = sem("square_ready"), sem("square_summed")
        s_psum, s_root, s_rstd = sem("post_summed"), sem("root_ready"), sem("rstd_ready")
        s_pr, s_ph, s_pl = sem("product_ready"), sem("product_hi"), sem("product_lo")
        s_x = sem("residual_updated")
        s_fsq = sem("branch_square_added")
        s_out = sem("out_stored")
        s_dch = sem("dve_chain")
        block = ctx.enter_context(nc.Block())

        def sb_tmp(b):
            return EV[:, b, :] if b < EV_RING else TA[:]

        def sum_bank(name):
            return PS[4 if name == "ssd1" else 5]

        def ssd_x(g, p):
            return row(XT, p) if g else row(XB, p + 4)

        @block.sync
        def _(sp):
            sp.dma_start(CO[:], consts).then_inc(s_in, 16)
            sp.dma_start(PA[:], params).then_inc(s_in, 16)
            sp.dma_start(ROPE_N[:], rope[:, 0:2, :]).then_inc(s_in, 16)
            sp.dma_start(WGR[:], w_gate).then_inc(s_in, 16)
            sp.dma_start(X[:], xT).then_inc(s_xin, 16)

            def load_stage(name):
                base, wide = SLOT0[name], sum(WIDTH[SLOT0[name]:SLOT0[name] + GROUP.get(name, 4)]) * P

                def body(s, i, g):
                    c = base + s
                    col = COL0[name] + sum(WIDTH[base:c]) * P
                    if c >= RAW_RING:
                        sp.wait_ge(s_lo, i * g + c - RAW_RING + 1)
                    sp.dma_start(WR[:, c % RAW_RING, 0:WIDTH[c] * P],
                                 w_all[:, bass.ds(i * wide + col, WIDTH[c] * P)]).then_inc(s_raw[c % RAW_RING], 16)
                run_stage(sp, name, body)

            load_stage("nsa_rope")
            for t in ("k", "v"):
                sp.dma_start(W1[t][:], w1k if t == "k" else w1v).then_inc(s_late["cmp_w"], 16)
                sp.dma_start(W2[t][:], w2k if t == "k" else w2v).then_inc(s_late["cmp_w"], 16)
            sp.dma_start(ROPE_R[:], rope[:, 2:4, :]).then_inc(s_late["rope_ret"], 16)
            for name in ("nsa_plain", "ret_in", "z_ret", "z_nsa", "merge", "out1", "ffn1_up",
                         "ffn1_down", "sb_qkv", "ssd_early", "ssd_late", "out2", "xa_q", "xa_kv", "xa_o", "ffn2_up",
                         "ffn2_down"):
                load_stage(name)
            for k in range(DK):
                sp.wait_ge(s_x, 4 * DK + k + 1)
                sp.dma_start(out_t[:, k, :], X[:, k, :]).then_inc(s_out, 16)
            sp.wait_ge(s_out, 16 * DK)

        @block.gpsimd
        def _(pool):
            nc.gpsimd.sem_inc(sem("ssd_rows"), 1)

            pool.wait_ge(sem("nsa_out"), NSA_PAIRS)
            pool.dma_start(RDEC[:], decay[:, 0, :]).then_inc(s_late["decay"], 16)
            with pool.Fori(1, RET_HEADS) as h:
                pool.wait_ge(sem("ret_decayed"), h * SC)
                pool.dma_start(RDEC[:], row(decay, h)).then_inc(s_late["decay"], 16)


            def keep_later(view, op, blocks):
                return nc.gpsimd.affine_select(out=view, in_=view, compare_op=op, fill=0.0, base=0,
                                               pattern=[[0, blocks], [1, P]], channel_multiplier=-1)

            def diagonals(tile, b):
                v = tile.rearrange("p (a c) -> p a c", c=P)
                return v[:, 0:1, :] if b < 2 else v[:, 0:4:3, :] if b < 4 else v[:, 0:4:2, :]

            with pool.Fori(0, SB_PAIRS) as p:
                for b in range(5):
                    wait_apart(pool, sem("sb_softplus"), p * 5 + b + 1, sem("pool_seen"))
                    keep_later(diagonals(SPB[:, b, :], b), ALU.is_gt, 1 if b < 2 else 2).then_inc(
                        sem("sb_softplus_masked"), 1)
                for b in range(5):
                    wait_apart(pool, sem("sb_exp"), p * 5 + b + 1, sem("pool_seen"))
                    keep_later(diagonals(sb_tmp(b), b), ALU.is_gt, 1 if b < 2 else 2).then_inc(
                        sem("sb_exp_masked"), 1)
            pool.wait_ge(sem("sb_out"), SB_PAIRS + 1)
            pool.dma_start(WDR[:], w_dt).then_inc(s_late["dt_w"], 16)
            for g in range(2):
                pool.wait_ge(sem("ssd_cb"), g + 1)
                keep_later(CBM[:, g], ALU.is_ge, SC).then_inc(sem("ssd_cb_masked"), 1)
            pool.wait_ge(sem("adt"), 1)
            for g in range(2):
                with pool.Fori(0, 4) as p:
                    heads = bass.ds(p * 2 + 8 * g, 2)
                    wait_apart(pool, sem("ssd_rows"), p + 4 * g + 1, sem("pool_seen"))
                    for c in range(SC):
                        nc.gpsimd.tensor_tensor(LSG[:, c], const("later").unsqueeze(1).broadcast_to([P, 2, P]),
                                                ADT[:, c, heads].unsqueeze(2).broadcast_to([P, 2, P]), ALU.mult)
                    nc.gpsimd.tensor_copy(ARP[:].rearrange("p c (h d) -> p c h d", h=2),
                                          ADT[:, :, heads].unsqueeze(3).broadcast_to([P, SC, 2, SSD_P])).then_inc(
                        sem("ssd_lhs"), 1)
            pool.wait_ge(s_x, 3 * DK)
            pool.dma_start(MR[:], mem_t).then_inc(s_late["mem"], 16)


        @block.scalar
        def _(act):
            A = nc.scalar.activation
            nc.scalar.sem_inc(sem("sb_out"), 1)

            def split_hi(c, i, g):
                nb = WIDTH[c]
                act.wait_ge(s_raw[c % RAW_RING], i * (16 * g // 4) + 16 * (c // RAW_RING + 1))
                if c >= HL_RING:
                    act.wait_ge(s_used, i * g + c - HL_RING + 1)
                A(WH[:, c % HL_RING, 0:nb * P], WR[:, c % RAW_RING, 0:nb * P], ACT.Copy).then_inc(s_hi, 1)

            def stage(name, tile, first_split=False):
                base, per = SLOT0[name], PER_TILE.get(name, 1)

                def body(s, i, g):
                    if base + s + 1 < N_SLOTS and not (first_split and s == 0):
                        split_hi(base + s + 1, i, g)
                    if s % per == per - 1:
                        act.wait_ge(s_used, i * g + base + s + 1)
                        tile(s // per, i, g // per)
                run_stage(act, name, body)

            def acc(name, t):
                return ACC[(TILE0[name] + t) % 2][:]

            def ev(name, t):
                return EV[:, (EV0[name] + t) % EV_RING, :]

            def squares(name, src, ready, n=S):
                q0 = SUM_SQ0[name]
                for k in range(SUMS[SUM_N[name]][1]):
                    ready(k)
                    if q0 + k >= 2:
                        act.wait_ge(s_squsd, q0 + k - 1)
                    A(SQ[:, (q0 + k) % 2, 0:n], src(k), ACT.Square).then_inc(s_sq, 1)

            def root(name, dim, n=S):
                j = SUM_N[name]
                if SUMS[j][1] > 1:
                    act.wait_ge(s_squsd, SUM_SQ0[name] + SUMS[j][1])
                else:
                    act.wait_ge(s_psum, POST[name] + 1)
                if j:
                    act.wait_ge(s_rstd, j)
                A(RM[:, 0:n], sum_bank(name)[:, 0:n], ACT.Sqrt, scale=1.0 / dim, bias=EPS).then_inc(s_root, 1)

            def product_hi(j, off, dst, n=S):
                act.wait_ge(s_pr, off + j + 1)
                A(dst, PR[:, j % 2, 0:n], ACT.Copy).then_inc(s_ph, 1)

            def norm_hi(name, dst, n=S, ks=range(DK)):
                for k in ks:
                    product_hi(PROD0[name] + k, 0, dst(k), n)

            def boundary(b, post, pre, prod):
                root(post, D)
                squares(pre, lambda k: X[:, k, :], lambda k: act.wait_ge(s_x, b * DK + k + 1))
                root(pre, D)
                norm_hi(prod, lambda k: HH[:, k, :])

            def branch(name):
                def tile(t, i, m):
                    A(row(FO, i * m + t), acc(name, t), ACT.Copy)
                    act.wait_ge(s_fsq, i * m + BRANCH[name] * DK + t + 1)
                    A(ev(name, t), acc(name, t), ACT.Square).then_inc(s_acc, 1)
                stage(name, tile)

            def plain(name, dst, n=S):
                stage(name, lambda t, i, m: A(row(dst, i * m + t), acc(name, t)[:, 0:n], ACT.Copy).then_inc(s_acc, 1))

            act.wait_ge(s_in, 64)
            A(WGH[:], WGR[:], ACT.Copy).then_inc(sem("gate_w_hi"), 1)
            act.wait_ge(s_xin, 16)
            squares("pre", lambda k: X[:, k, :], lambda k: None)
            root("pre", D)
            split_hi(0, 0, 4)
            norm_hi("norm_pre", lambda k: HH[:, k, :])

            def nsa_rope_tile(t, i, m):
                if t >= EV_RING:
                    act.wait_ge(sem("nsa_roped"), t - EV_RING + 1)
                A(ev("nsa_rope", t), acc("nsa_rope", t), ACT.Copy).then_inc(s_acc, 1)
            stage("nsa_rope", nsa_rope_tile)
            plain("nsa_plain", VN)

            act.wait_ge(sem("gate_rows"), 1)
            A(NROWS[0:24, :], PS[2][0:24, :], ACT.Copy).then_inc(sem("gate_rows_copied"), 1)
            act.wait_ge(sem("gate_sum"), 1)
            A(GT[:], GT[:], ACT.Sigmoid).then_inc(sem("gate_ready"), 1)
            for n, t in enumerate(("k", "v")):
                act.wait_ge(sem("cmp_hidden"), n + 1)
                A(HG[t][:], PS[n][:, 0:4 * N_CMP].rearrange("p (j c) -> p j c", j=2),
                  ACT.Gelu_apprx_tanh).then_inc(sem("cmp_gelu"), 1)

            def ret_in_leaves(p, s):
                act.wait_ge(s_used, p * 4 + SLOT0["ret_in"] + s + 1)
                if s < 2:
                    act.wait_ge(sem("ret_roped"), p * 2 + s + 1)
                dst = EV[:, s, :] if s < 2 else row(RV, p * 2 + s - 2)
                A(dst, ACC[(TILE0["ret_in"] + s) % 2][:], ACT.Copy).then_inc(s_acc, 1)

            with act.Fori(0, NSA_PAIRS) as p:
                for u in range(8):
                    kw = (u // 2 + 1) * P
                    act.wait_ge(sem("nsa_max"), p * 8 + u + 1)
                    A(PB[:, 0:kw], PS[0][:, 0:kw], ACT.Exp, bias=NM[:, 1:2], scale=NSA_SCALE, accum_out=SU[:, 1:2])
                    A(PB[:, S:S + kw], PS[1][:, 0:kw], ACT.Exp, bias=NM[:, 2:3], scale=NSA_SCALE,
                      accum_out=SU[:, 2:3])
                    A(PB[:, 2 * S:2 * S + N_CMP], PS[2][:, 0:N_CMP], ACT.Exp, bias=NM[:, 0:1],
                      scale=NSA_SCALE).then_inc(sem("nsa_exp"), 1)
                    act.wait_ge(sem("nsa_turned"), p * 8 + u + 1)
                    A(PTS[:, 0:kw // P, :], PS[3][:, 0:kw].rearrange("p (c t) -> p c t", t=P),
                      ACT.Copy).then_inc(sem("nsa_sel_t"), 1)
                    if u % 2 == 0:
                        if u:
                            ret_in_leaves(p, u // 2 - 1)
                        split_hi(SLOT0["ret_in"] + u // 2 + 1, p, 4)
                act.wait_ge(sem("nsa_pv"), p * 8 + 8)
                A(row(OA, p), PS[5][:], ACT.Copy).then_inc(sem("nsa_out"), 1)
                ret_in_leaves(p, 3)

            act.wait_ge(sem("ret_roped"), 2 + 8)

            def gate_leaves(h, i, c):
                wait_apart(act, s_used, i * 4 + SLOT0["z_ret"] + c + 1, sem("act_seen"))
                A(row(RV, h * 2 + c % 2), ACC[(TILE0["z_ret"] + c) % 2][:], ACT.Copy).then_inc(s_acc, 1)

            def ret_head(i, q):
                h = i * 2 + q
                A(EV[:, 0:2, :], RV[:, bass.ds(h * 2, 2), :], ACT.Copy).then_inc(sem("ret_v_staged"), 1)
                act.wait_ge(sem("ret_pv"), h + 1)
                for e in range(2):
                    A(row(ORT, h * 2 + e), PS[3 + e][:], ACT.Copy).then_inc(sem("ret_raw"), 1)
                for e in range(2):
                    wait_apart(act, sem("ret_centred"), h * 2 + e + 1, sem("act_seen"))
                    A(EV[:, 2 + e, :], row(ORT, h * 2 + e), ACT.Square).then_inc(sem("ret_sq"), 1)
                split_hi(SLOT0["z_ret"] + 2 * q + 1, i, 4)
                gate_leaves(h, i, 2 * q)
                act.wait_ge(sem("ret_var"), h + 1)
                A(TA[:], PS[1][:], ACT.Sqrt, bias=EPS).then_inc(sem("ret_root"), 1)
                split_hi(SLOT0["z_ret"] + 2 * q + 2, i, 4)
                gate_leaves(h, i, 2 * q + 1)
            with act.Fori(0, RET_HEADS // 2) as i:
                for q in range(2):
                    ret_head(i, q)

            def z_nsa_tile(t, i, m):
                for k in (2 * t, 2 * t + 1):
                    A(RV[:, k, :], RV[:, k, :], ACT.Silu).then_inc(sem("z_ret_silu"), 1)
                A(ev("z_nsa", t), acc("z_nsa", t), ACT.Silu).then_inc(s_acc, 1)
                for u, dst in enumerate((GRH[:, 2 * t, :], GRH[:, 2 * t + 1, :], GAH[:, t, :])):
                    product_hi(PROD0["gates"] + 3 * t + u, 0, dst)
            stage("z_nsa", z_nsa_tile)

            def merge_tile(t, i, m):
                A(ev("merge", t), acc("merge", t), ACT.Copy if t % 2 else ACT.Sigmoid).then_inc(s_acc, 1)
                if t % 4 == 3:
                    product_hi(PROD0["merge"] + t // 4, i * 2, row(MGH, i * 2 + t // 4))
            stage("merge", merge_tile)
            branch("out1")
            boundary(0, "post1", "ffn1", "norm_ffn1")

            def ffn(n):
                up = f"ffn{n}_up"

                def tile(t, i, m):
                    A(ev(up, t), acc(up, t), ACT.Copy if t % 2 else ACT.Silu).then_inc(s_acc, 1)
                    if t % 2:
                        product_hi(PROD0[f"ffn{n}"] + t // 2, i * 2, row(AH, i * 2 + t // 2))
                stage(up, tile)
                branch(f"ffn{n}_down")
            ffn(1)
            boundary(1, "post_ffn1", "mix", "norm_mix")

            plain("sb_qkv", QKV)
            early, late = SLOT0["ssd_early"], TILE0["ssd_late"]
            split_hi(early + 1, 0, 4)

            def sb_pair(i, q):
                p, s = i * 2 + q, 2 * q
                for b in range(5):
                    act.wait_ge(sem("sb_scored"), p * 5 + b + 1)
                    A(sb_tmp(b), PS[b][:], ACT.Abs).then_inc(sem("sb_abs"), 1)
                for b in range(5):
                    act.wait_ge(sem("sb_abs"), p * 5 + b + 1)
                    A(sb_tmp(b), sb_tmp(b), ACT.Exp, scale=-1.0).then_inc(sem("sb_neg_exp"), 1)
                for b in range(5):
                    act.wait_ge(sem("sb_neg_exp"), p * 5 + b + 1)
                    A(sb_tmp(b), sb_tmp(b), ACT.Ln, bias=1.0).then_inc(sem("sb_log"), 1)
                split_hi(early + s + 2, i, 4)
                act.wait_ge(sem("conv_sum"), p + 1)
                A(CR[:, q, :], ACC[(TILE0["ssd_early"] + s) % 2][:], ACT.Copy).then_inc(s_acc, 1)
                split_hi(early + s + 3, i, 4)
                act.wait_ge(s_used, i * 4 + early + s + 2)
                A(row(ZS, p), ACC[(TILE0["ssd_early"] + s + 1) % 2][:], ACT.Copy).then_inc(s_acc, 1)
                for b in range(5):
                    act.wait_ge(sem("sb_suffixed"), p * 5 + b + 1)
                    A(sb_tmp(b), PS[b][:], ACT.Exp).then_inc(sem("sb_exp"), 1)
                act.wait_ge(sem("sb_pv"), p + 1)
                A(row(OSB, p), PS[5][:], ACT.Copy).then_inc(sem("sb_out"), 1)
            with act.Fori(0, SB_PAIRS // 2) as i:
                for q in range(2):
                    sb_pair(i, q)
            act.wait_ge(sem("conv_sum"), 2 + 8)
            squares("attn", lambda k: OSB[:, k, :], lambda k: act.wait_ge(sem("sb_out"), SB_PAIRS + 1))
            root("attn", D)

            def conv_silu(t, view):
                act.wait_ge(sem("conv_sum"), 2 + t + 1)
                A(view, view, ACT.Silu).then_inc(sem("conv_silu"), 1)
            for t in range(8):
                conv_silu(t, XB[:, t, :])
            act.wait_ge(s_late["dt_w"], 16)
            A(WDH[:], WDR[:], ACT.Copy).then_inc(sem("dt_w_hi"), 1)

            def late_tile(t, i, m):
                act.wait_ge(sem("conv_sum"), 8 + t + 1)
                A(CR[:, t % 2, :], ACC[(TILE0["ssd_late"] + t) % 2][:], ACT.Copy).then_inc(s_acc, 1)
                norm_hi("norm_attn", lambda k: OSH[:, k, :], ks=(2 * t, 2 * t + 1))
            stage("ssd_late", late_tile, first_split=True)
            for t in range(4):
                conv_silu(8 + t, XT[:, t, :])
            for k in range(DK):
                A(ZS[:, k, :], ZS[:, k, :], ACT.Silu).then_inc(sem("z_silu"), 1)
            A(EAL[:], par("a_log", 0, SSD_HEADS), ACT.Exp).then_inc(sem("a_exp"), 1)
            act.wait_ge(sem("dt_rows"), 1)
            A(NROWS[0:SSD_HEADS, :], PS[0][0:SSD_HEADS, :], ACT.Copy).then_inc(sem("dt_rows_copied"), 1)
            act.wait_ge(sem("dt_in"), 1)
            A(DTL[:], DTX[:], ACT.Abs).then_inc(sem("dt_log"), 1)
            act.wait_ge(sem("dt_log"), 1)
            A(DTL[:], DTL[:], ACT.Exp, scale=-1.0).then_inc(sem("dt_log"), 1)
            act.wait_ge(sem("dt_log"), 2)
            A(DTL[:], DTL[:], ACT.Ln, bias=1.0).then_inc(sem("dt_log"), 1)
            act.wait_ge(sem("dt_sums"), 1)
            A(DEND[:], PS[1][:, 0:64].rearrange("p (c h) -> p c h", c=SC), ACT.Exp)
            A(CDEC[:], PS[2][:, 0:64].rearrange("p (c h) -> p c h", c=SC), ACT.Exp).then_inc(sem("dt_decays"), 1)
            for g in range(2):
                act.wait_ge(sem("ssd_bt"), g + 1)
                A(BTK[:, g], PS[3 + g][:].rearrange("p (c n) -> p c n", c=SC), ACT.Copy).then_inc(sem("ssd_b_tokens"), 1)
            for g in range(2):
                with act.Fori(0, 4) as p:
                    act.wait_ge(sem("ssd_seg"), p + 4 * g + 1)
                    for hh in range(2):
                        A(LM[:, hh], PS[1 + hh][:].rearrange("p (c t) -> p c t", c=SC), ACT.Exp).then_inc(
                            sem("ssd_seg_exp"), 1)
                    act.wait_ge(sem("ssd_rows"), p + 4 * g + 2)
                    act.wait_ge(sem("ssd_done"), p + 4 * g + 1)
                    A(ERW[:, P:S], PS[3][:, P:S], ACT.Exp).then_inc(sem("ssd_row_exp"), 1)

            for g in range(2):
                squares(f"ssd{g}", lambda k: (XT[:, k, :] if g else XB[:, 4 + k, :]),
                        lambda k: act.wait_ge(sem("ssd_done"), 9))
            for g in range(2):
                root(f"ssd{g}", D // 2)
            norm_hi("norm_ssd", lambda k: YSH[:, k, :])
            branch("out2")
            boundary(2, "post_mix", "xa", "norm_xa")

            plain("xa_q", XQ)
            act.wait_ge(s_late["mem"], 16)
            squares("mem", lambda k: MR[:, k, :], lambda k: None, MEM)
            root("mem", D, MEM)
            norm_hi("norm_mem", lambda k: MH[:, k, :], MEM)
            plain("xa_kv", XKV, MEM)

            def xa_exps(h):
                act.wait_ge(sem("xa_max"), h + 1)
                for i in range(SC):
                    A(CP[:, i, :], PS[1 + i // 2][:, (i % 2) * MEM:(i % 2 + 1) * MEM], ACT.Exp,
                      bias=CNM[:, i:i + 1], scale=XA_DH ** -0.5, accum_out=CSU[:, i:i + 1]).then_inc(sem("xa_exp"), 1)

            def xa_head(h, more):
                for mc in range(2):
                    act.wait_ge(sem("xa_turned"), h * 2 + mc + 1)
                    A(CPT[:, mc, :], PS[3 + mc][:], ACT.Copy).then_inc(sem("xa_probs_t"), 1)
                if more:
                    xa_exps(h + 1)
                for e in range(2):
                    product_hi(PROD0["xa"] + e, h * 2, row(XOH, h * 2 + e))
            xa_exps(0)
            with act.Fori(0, XA_HEADS - 1) as h:
                xa_head(h, True)
            xa_head(XA_HEADS - 1, False)
            branch("xa_o")
            boundary(3, "post_xa", "ffn2", "norm_ffn2")
            ffn(2)
            root("post_ffn2", D)

        @block.vector
        def _(dve):
            V = nc.vector
            TT, TS, STT = V.tensor_tensor, V.tensor_scalar, V.scalar_tensor_tensor
            chain = Tally(dve, s_dch)
            V.sem_inc(s_fsq, EV_RING)
            V.sem_inc(sem("ret_roped"), 2)
            V.sem_inc(sem("conv_sum"), 2)
            V.sem_inc(sem("ssd_done"), 1)

            def split_lo(c, i, g):
                nb = WIDTH[c]
                dve.wait_ge(s_hi, i * g + c + 1)
                TT(WL[:, c % HL_RING, 0:nb * P], WR[:, c % RAW_RING, 0:nb * P],
                   WH[:, c % HL_RING, 0:nb * P].bitcast(F32), ALU.subtract).then_inc(s_lo, 1)

            def stage(name, tile=None, per=None, first_split=False):
                base, per = SLOT0[name], per or PER_TILE.get(name, 1)

                def body(s, i, g):
                    if base + s + 1 < N_SLOTS and not (first_split and s == 0):
                        split_lo(base + s + 1, i, g)
                    if tile is not None and s % per == per - 1:
                        tiles = g // PER_TILE.get(name, 1)
                        t = s // PER_TILE.get(name, 1)
                        dve.wait_ge(s_acc, i * tiles + TILE0[name] + t + 1)
                        tile(s // per, i, g // per)
                run_stage(dve, name, body)

            def ev(name, t):
                return EV[:, (EV0[name] + t) % EV_RING, :]

            def free_product(j, off):
                if j >= 2:
                    dve.wait_ge(s_pl, off + j - 1)

            def low(j, off, hi, lo, n=S):
                dve.wait_ge(s_ph, off + j + 1)
                TT(lo, PR[:, j % 2, 0:n], hi.bitcast(F32), ALU.subtract).then_inc(s_pl, 1)

            def rstd(name, n=S):
                j = SUM_N[name]
                dve.wait_ge(s_root, j + 1)
                V.reciprocal(RS[:, 0:n], RM[:, 0:n]).then_inc(s_rstd, 1)
                dve.wait_ge(s_rstd, j + 1)

            def apply_norm(name, src, gain, hi, lo, n=S, ks=range(DK)):
                def make(k):
                    j = PROD0[name] + k
                    free_product(j, 0)
                    STT(out=PR[:, j % 2, 0:n], in0=src(k), scalar=par(gain, k), in1=RS[:, 0:n], op0=ALU.mult,
                        op1=ALU.mult).then_inc(s_pr, 1)
                make(ks[0])
                for k in ks:
                    if k + 1 in ks:
                        make(k + 1)
                    low(PROD0[name] + k, 0, hi(k), lo(k), n)

            def norm(total, name, gain):
                rstd(total)
                apply_norm(name, lambda k: X[:, k, :], gain, lambda k: HH[:, k, :], lambda k: HL[:, k, :])

            def branch(name):
                def add_square(t, i, m):
                    TT(SSQ[:], SSQ[:], ev(name, t), ALU.add).then_inc(s_fsq, 1)
                    dve.wait_ge(s_fsq, i * m + BRANCH[name] * DK + EV_RING + t + 1)
                chain.link(V.memset(SSQ[:], 0.0))
                stage(name, add_square)

            def boundary(b, post, gain, factor):
                rstd(post)

                def scaled(k):
                    STT(out=FO[:, k, :], in0=FO[:, k, :], scalar=par(gain, k), in1=RS[:], op0=ALU.mult,
                        op1=ALU.mult).then_inc(sem("branch_scaled"), 1)
                scaled(0)
                for k in range(DK):
                    if k + 1 < DK:
                        scaled(k + 1)
                    dve.wait_ge(sem("branch_scaled"), b * DK + k + 1)
                    STT(out=X[:, k, :], in0=FO[:, k, :], scalar=factor, in1=X[:, k, :], op0=ALU.mult,
                        op1=ALU.add).then_inc(s_x, 1)

            dve.wait_ge(sem("gate_w_hi"), 1)
            TT(WGL[:], WGR[:], WGH[:].bitcast(F32), ALU.subtract).then_inc(sem("gate_w_lo"), 1)
            split_lo(0, 0, 4)
            norm("pre", "norm_pre", "g_pre")

            def nsa_rope_tile(t, i, m):
                chain.link(TT(TB[:], ev("nsa_rope", t), ROPE_N[:, 0, :], ALU.mult))
                dve.wait_ge(sem("nsa_turned_half"), t + 1)
                chain.link(TT(TA[:], PS[t % 2][:], ROPE_N[:, 1, :], ALU.mult))
                TT(QK[:, t, :], TA[:], TB[:], ALU.add).then_inc(sem("nsa_roped"), 1)
                dve.wait_ge(sem("nsa_roped"), t + 1)
            last = COUNT["nsa_rope"] - 1
            stage("nsa_rope", lambda t, i, m: nsa_rope_tile(t - 1, i, m) if t else None)
            stage("nsa_plain", lambda t, i, m: nsa_rope_tile(last, i, m) if t == 0 else None)

            for t, src in (("k", QK[:, 4, :]), ("v", VN[:, 0, :])):
                if t == "v":
                    dve.wait_ge(s_acc, TILE0["nsa_plain"] + 3)
                for g in range(2):
                    kv = src[64 * g:64 * g + 64, :].rearrange("p (m b r) -> p m b r", b=8, r=2)
                    for r in range(2):
                        for a in range(2):
                            pe_at = PCOL["pe_" + t][0] + r * 16 + a * 8
                            last = TT(BLK[t][64 * r:64 * r + 64, 8 * a:8 * a + 8, g * N_CMP:(g + 1) * N_CMP],
                                      kv[:, a:a + N_CMP, :, r].rearrange("p m b -> p b m"),
                                      PA[64 * g:64 * g + 64, pe_at:pe_at + 8].unsqueeze(2).broadcast_to(
                                          [64, 8, N_CMP]), ALU.add)
                last.then_inc(sem("cmp_blocks"), 1)

            dve.wait_ge(sem("gate_psum"), 1)
            TT(GT[:], PS[2][:, 0:SC * 24].rearrange("p (c h) -> p c h", c=SC),
               par("gate_b", 0, 24).unsqueeze(1).broadcast_to([P, SC, 24]), ALU.add).then_inc(sem("gate_sum"), 1)
            for n, dst in enumerate((VS, VW)):
                dve.wait_ge(sem("nsa_v_turned"), n + 1)
                V.tensor_copy(dst[:], PS[3 + n][:].rearrange("p (c f) -> p c f", c=SC)).then_inc(sem("nsa_v_tokens"), 1)
            dve.wait_ge(sem("cmp_done"), 1)
            V.tensor_copy(KCT[:, 0:N_CMP], PS[2][:, 0:N_CMP])
            V.tensor_copy(VCT[0:N_CMP, :, :], PS[2][0:N_CMP, P:2 * P].rearrange("p (g d) -> p g d", g=2)).then_inc(
                sem("cmp_kv"), 1)

            dve.wait_ge(s_late["rope_ret"], 16)

            def ret_rotate(p, s):
                dve.wait_ge(s_acc, p * 4 + TILE0["ret_in"] + s + 1)
                e, t = EV[:, s, :], p * 2 + s
                dve.wait_ge(sem("ret_roped"), t + 2)
                TT(TA[0:64, :], e[64:128, :], ROPE_R[64:128, 1, :], ALU.mult)
                TT(TA[64:128, :], e[0:64, :], ROPE_R[0:64, 1, :], ALU.mult)
                TT(TB[:], e, ROPE_R[:, 0, :], ALU.mult).then_inc(sem("ret_rope_parts"), 1)
                dve.wait_ge(sem("ret_rope_parts"), t + 1)
                TT(row(RQK, t), TA[:], TB[:], ALU.add).then_inc(sem("ret_roped"), 1)
            with dve.Fori(0, NSA_PAIRS) as p:
                chain.enter(p, 8 * 6)
                V.tensor_copy(QST[:], row(QK, p)).then_inc(sem("nsa_staged"), 1)
                for u in range(8):
                    i, hh = divmod(u, 2)
                    kw = (i + 1) * P
                    dve.wait_ge(sem("nsa_scored"), p * 8 + u + 1)
                    V.reduce_max(MX[:, 1:2], PS[0][:, 0:kw], AX)
                    V.reduce_max(MX[:, 2:3], PS[1][:, 0:kw], AX)
                    chain.link(V.reduce_max(MX[:, 0:1], PS[2][:, 0:N_CMP], AX))
                    TS(NM[:, 0:3], MX[:, 0:3], -NSA_SCALE, None, ALU.mult).then_inc(sem("nsa_max"), 1)
                    if u % 2:
                        split_lo(SLOT0["ret_in"] + u // 2 + 1, p, 4)
                    dve.wait_ge(sem("nsa_exp"), p * 8 + u + 1)
                    pc = PB[:, 2 * S:2 * S + N_CMP]
                    keep = const("cmp_keep")[:, i * 32:i * 32 + N_CMP]
                    chain.link(TT(pc, pc, keep, ALU.mult))
                    chain.link(V.reduce_sum(SU[:, 0:1], pc, AX))
                    chain.link(TS(SU[:, 0:3], SU[:, 0:3], TINY, None, ALU.max))
                    chain.link(V.reciprocal(SR[:, 0:3], SU[:, 0:3]))
                    chain.link(TT(SW[:, 0:3], SR[:, 0:3], GT[:, i, bass.ds(p * 3 + 12 * hh, 3)], ALU.mult))
                    TS(pc, pc, SW[:, 0:1], None, ALU.mult)
                    TS(PB[:, 0:kw], PB[:, 0:kw], SW[:, 1:2], None, ALU.mult)
                    TS(PB[:, S:S + kw], PB[:, S:S + kw], SW[:, 2:3], None, ALU.mult).then_inc(sem("nsa_scaled"), 1)
                    if u in (3, 5):
                        ret_rotate(p, u // 2 - 1)
                    dve.wait_ge(sem("nsa_turned"), p * 8 + u + 1)
                    V.tensor_copy(PTC[0:N_CMP, :], PS[2][0:N_CMP, P:2 * P])
                    V.tensor_copy(PTW[:, 0:i + 1, :], PS[4][:, 0:kw].rearrange("p (c t) -> p c t", t=P)).then_inc(
                        sem("nsa_win_t"), 1)
                dve.wait_ge(sem("nsa_out"), p + 1)
                chain.leave(NSA_PAIRS)

            z_ret = SLOT0["z_ret"]

            def ret_head(i, q):
                h = i * 2 + q
                V.tensor_copy(RQS[:], row(RQK, h))
                V.tensor_copy(RKS[:], row(RQK, h + RET_HEADS)).then_inc(sem("ret_staged"), 1)
                for e in range(2):
                    dve.wait_ge(sem("ret_v_turned"), h * 2 + e + 1)
                    V.tensor_copy(RVT[:, :, e * P:(e + 1) * P], PS[e][:].rearrange("p (c f) -> p c f", c=SC)).then_inc(
                        sem("ret_v_tokens"), 1)
                dve.wait_ge(s_late["decay"], h * 16 + 16)
                for j in range(SC):
                    w = S - j * P
                    dve.wait_ge(sem("ret_scored"), h * SC + j + 1)
                    TT(RSM[:, j, 0:w], PS[(2, 5)[j % 2]][:, 0:w], RDEC[:, 0:w], ALU.mult).then_inc(sem("ret_decayed"), 1)
                for e in range(2):
                    o = row(ORT, h * 2 + e)
                    if e == 0:
                        dve.wait_ge(sem("ret_mean"), h + 1)
                    TT(o, o, PS[0][:], ALU.subtract).then_inc(sem("ret_centred"), 1)
                split_lo(z_ret + 2 * q + 1, i, 4)
                dve.wait_ge(sem("ret_root"), h + 1)
                V.reciprocal(TB[:], TA[:]).then_inc(sem("ret_rstd"), 1)
                split_lo(z_ret + 2 * q + 2, i, 4)
                dve.wait_ge(sem("ret_rstd"), h + 1)
                dve.wait_ge(sem("ret_centred"), h * 2 + 2)
                TT(row(ORT, h * 2), row(ORT, h * 2), TB[:], ALU.mult)
                TT(row(ORT, h * 2 + 1), row(ORT, h * 2 + 1), TB[:], ALU.mult).then_inc(sem("ret_done"), 1)
            with dve.Fori(0, RET_HEADS // 2) as i:
                for q in range(2):
                    ret_head(i, q)

            dve.wait_ge(sem("ret_done"), RET_HEADS)

            def z_nsa_tile(t, i, m):
                made = ((ORT[:, 2 * t, :], RV[:, 2 * t, :], GRH[:, 2 * t, :], GRL[:, 2 * t, :]),
                        (ORT[:, 2 * t + 1, :], RV[:, 2 * t + 1, :], GRH[:, 2 * t + 1, :], GRL[:, 2 * t + 1, :]),
                        (OA[:, t, :], ev("z_nsa", t), GAH[:, t, :], GAL[:, t, :]))
                for u, (value, gate, hi, lo) in enumerate(made):
                    j = PROD0["gates"] + 3 * t + u
                    if u < 2:
                        dve.wait_ge(sem("z_ret_silu"), 2 * t + u + 1)
                    free_product(j, 0)
                    TT(PR[:, j % 2, :], value, gate, ALU.mult).then_inc(s_pr, 1)
                    low(j, 0, hi, lo)
            stage("z_nsa", z_nsa_tile)

            def merge_tile(t, i, m):
                e = [ev("merge", 4 * t + u) for u in range(4)]
                j = PROD0["merge"] + t
                TT(TA[:], e[0], e[1], ALU.mult).then_inc(sem("merge_parts"), 1)
                TT(TB[:], e[2], e[3], ALU.mult).then_inc(sem("merge_parts"), 1)
                dve.wait_ge(sem("merge_parts"), (i * m + t) * 2 + 2)
                free_product(j, i * m)
                TT(PR[:, j % 2, :], TA[:], TB[:], ALU.add).then_inc(s_pr, 1)
                low(j, i * m, row(MGH, i * m + t), row(MGL, i * m + t))
            stage("merge", merge_tile, per=4)
            branch("out1")
            boundary(0, "post1", "g_post", 1.0)
            norm("ffn1", "norm_ffn1", "g_ffn1_pre")

            def ffn(n):
                def tile(t, i, m):
                    j = PROD0[f"ffn{n}"] + t
                    free_product(j, i * m)
                    TT(PR[:, j % 2, :], ev(f"ffn{n}_up", 2 * t), ev(f"ffn{n}_up", 2 * t + 1), ALU.mult).then_inc(s_pr, 1)
                    low(j, i * m, row(AH, i * m + t), row(AL, i * m + t))
                stage(f"ffn{n}_up", tile, per=2)
                branch(f"ffn{n}_down")
            ffn(1)
            boundary(1, "post_ffn1", "g_ffn1_post", 0.5)
            norm("mix", "norm_mix", "g_mix_pre")

            stage("sb_qkv")
            dve.wait_ge(s_acc, TILE0["ssd_early"])
            early = SLOT0["ssd_early"]
            split_lo(early + 1, 0, 4)

            def conv(t, raw, dst):
                def column(name, k=0):
                    a = PCOL[name][0] + k * CONV_TILES
                    return PA[:, bass.ds(t + a, 1)]
                chained, n = sem("conv_chain"), t * 3
                dve.wait_ge(sem("conv_sum"), t + 2)
                TS(TB[:], raw, column("conv_w", 3), column("conv_b"), ALU.mult, ALU.add).then_inc(chained, 1)
                for k in (1, 2):
                    dve.wait_ge(chained, n + k)
                    STT(out=TB[:, k:S], in0=raw[:, 0:S - k], scalar=column("conv_w", 3 - k), in1=TB[:, k:S],
                        op0=ALU.mult, op1=ALU.add).then_inc(chained, 1)
                dve.wait_ge(chained, n + 3)
                STT(out=dst[:, 3:S], in0=raw[:, 0:S - 3], scalar=column("conv_w", 0), in1=TB[:, 3:S], op0=ALU.mult,
                    op1=ALU.add)
                V.tensor_copy(dst[:, 0:3], TB[:, 0:3]).then_inc(sem("conv_sum"), 1)

            def sb_pair(i, q):
                p, s = i * 2 + q, 2 * q
                TS(BQS[:], row(QKV, p), DH ** -0.5, None, ALU.mult)
                V.tensor_copy(BKS[:], row(QKV, p + 8))
                V.tensor_copy(BVS[:], row(QKV, p + 16)).then_inc(sem("sb_staged"), 1)
                dve.wait_ge(sem("sb_v_turned"), p + 1)
                V.tensor_copy(BVT[:], PS[5][:].rearrange("p (c f) -> p c f", c=SC)).then_inc(sem("sb_v_tokens"), 1)
                for b in range(5):
                    dve.wait_ge(sem("sb_log"), p * 5 + b + 1)
                    STT(out=SPB[:, b, :], in0=PS[b][:], scalar=0.0, in1=sb_tmp(b), op0=ALU.max, op1=ALU.add).then_inc(
                        sem("sb_softplus"), 1)
                split_lo(early + s + 2, i, 4)
                dve.wait_ge(s_acc, i * 4 + TILE0["ssd_early"] + s + 1)
                conv(p, CR[:, q, :], row(XB, p))
                split_lo(early + s + 3, i, 4)
            with dve.Fori(0, SB_PAIRS // 2) as i:
                for q in range(2):
                    sb_pair(i, q)

            dve.wait_ge(sem("sb_out"), SB_PAIRS + 1)
            rstd("attn")
            dve.wait_ge(sem("dt_w_hi"), 1)
            TT(WDL[:], WDR[:], WDH[:].bitcast(F32), ALU.subtract).then_inc(sem("dt_w_lo"), 1)

            def late_tile(t, i, m):
                conv(8 + t, CR[:, t % 2, :], XT[:, t, :])
                apply_norm("norm_attn", lambda k: OSB[:, k, :], "g_attn", lambda k: OSH[:, k, :],
                           lambda k: OSL[:, k, :], ks=(2 * t, 2 * t + 1))
            stage("ssd_late", late_tile, first_split=True)
            dve.wait_ge(sem("dt_psum"), 1)
            TT(DTX[:], PS[0][:, 0:SC * SSD_HEADS].rearrange("p (c h) -> p c h", c=SC),
               par("dt_b", 0, SSD_HEADS).unsqueeze(1).broadcast_to([P, SC, SSD_HEADS]), ALU.add).then_inc(sem("dt_in"), 1)
            dve.wait_ge(sem("dt_log"), 3)
            chain.link(STT(out=DT[:], in0=DTX[:], scalar=0.0, in1=DTL[:], op0=ALU.max, op1=ALU.add))
            dve.wait_ge(sem("a_exp"), 1)
            STT(out=ADT[:], in0=DT[:], scalar=-1.0, in1=EAL[:].unsqueeze(1).broadcast_to([P, SC, SSD_HEADS]),
                op0=ALU.mult, op1=ALU.mult).then_inc(sem("adt"), 1)
            for g in range(2):
                dve.wait_ge(sem("ssd_cb_psum"), g + 1)
                V.tensor_copy(CBM[:, g], PS[(5, 0)[g]][:].rearrange("p (c t) -> p c t", c=SC)).then_inc(sem("ssd_cb"), 1)
            dve.wait_ge(sem("dt_decays"), 1)
            dve.wait_ge(sem("adt"), 1)
            dve.wait_ge(sem("conv_silu"), CONV_TILES)
            dve.wait_ge(sem("z_silu"), DK)
            for g in range(2):
                dve.wait_ge(sem("ssd_cb_masked"), g + 1)
                with dve.Fori(0, 4) as p:
                    chain.enter(p, 8)
                    n = p + 4 * g
                    heads = bass.ds(p * 2 + 8 * g, 2)

                    def by_head(t, c0, c1, width):
                        return t[:, c0:c1, heads].unsqueeze(3).broadcast_to([P, c1 - c0, 2, width])
                    V.tensor_copy(XST, ssd_x(g, p)).then_inc(sem("ssd_staged"), 1)
                    dve.wait_ge(sem("ssd_x_turned"), n + 1)
                    chain.link(TT(X1[:], PS[0][:].rearrange("p (c h d) -> p c h d", c=SC, h=2),
                                  by_head(DT, 0, SC, SSD_P), ALU.mult))
                    TT(X2[:], X1[:], by_head(DEND, 0, SC, SSD_P), ALU.mult).then_inc(sem("ssd_x12"), 1)
                    for hh in range(2):
                        dve.wait_ge(sem("ssd_seg_exp"), n * 2 + hh + 1)
                        TT(LM[:, hh], LM[:, hh], CBM[:, g], ALU.mult).then_inc(sem("ssd_m"), 1)
                    dve.wait_ge(sem("ssd_new"), n + 1)
                    chain.link(V.tensor_copy(STT_[:, 0, :], PS[4][:, 0:P]))
                    for c in (1, 2):
                        chain.link(TT(STT_[:, c, :].rearrange("p (h d) -> p h d", h=2),
                                      STT_[:, c - 1, :].rearrange("p (h d) -> p h d", h=2),
                                      CDEC[:, c, heads].unsqueeze(2).broadcast_to([P, 2, SSD_P]), ALU.mult))
                        ins = TT(STT_[:, c, :], STT_[:, c, :], PS[4][:, c * P:(c + 1) * P], ALU.add)
                        if c == 1:
                            chain.link(ins)
                        else:
                            ins.then_inc(sem("ssd_states"), 1)
                    dve.wait_ge(sem("ssd_y"), n + 1)
                    d_at = PCOL["d_skip"][0] + 4 * g
                    d_col, x = PA[:, bass.ds(p + d_at, 1)], ssd_x(g, p)
                    chain.link(STT(out=TA[:], in0=x, scalar=d_col, in1=PS[5][:], op0=ALU.mult, op1=ALU.add))
                    dve.wait_ge(sem("ssd_row_exp"), n + 1)
                    chain.link(TT(TB[:, P:S], ERW[:, P:S], PS[0][:, P:S], ALU.mult))
                    chain.link(TT(TA[:, P:S], TA[:, P:S], TB[:, P:S], ALU.add))
                    TT(x, TA[:], row(ZS, n), ALU.mult).then_inc(sem("ssd_done"), 1)
                    chain.leave(4)
            dve.wait_ge(sem("ssd_done"), 9)
            for g in range(2):
                rstd(f"ssd{g}")
                apply_norm("norm_ssd", lambda k: XT[:, k - 4, :] if k >= 4 else XB[:, 4 + k, :], "g_ssd", lambda k: YSH[:, k, :],
                           lambda k: YSL[:, k, :], ks=range(4 * g, 4 * g + 4))
            branch("out2")
            boundary(2, "post_mix", "g_mix_post", 1.0)
            norm("xa", "norm_xa", "g_xa_pre")

            stage("xa_q")
            rstd("mem", MEM)
            apply_norm("norm_mem", lambda k: MR[:, k, :], "g_mem", lambda k: MH[:, k, :], lambda k: ML[:, k, :], MEM)
            stage("xa_kv")
            dve.wait_ge(s_acc, TILE0["xa_o"])

            def xa_stage(h):
                V.tensor_copy(CQS[:], XQ[:, bass.ds(h * 2, 2), :])
                V.tensor_copy(CKS[:], XKV[:, bass.ds(h * 2, 2), :])
                V.tensor_copy(CVS[:], XKV[:, bass.ds(h * 2 + 8, 2), :]).then_inc(sem("xa_staged"), 1)

            def xa_maxima(h):
                dve.wait_ge(sem("xa_scored"), h + 1)
                for a in range(2):
                    ins = V.reduce_max(CMX[:, 2 * a:2 * a + 2], PS[1 + a][:].rearrange("p (i m) -> p i m", i=2), AX)
                chain.link(ins)
                TS(CNM[:], CMX[:], -(XA_DH ** -0.5), None, ALU.mult).then_inc(sem("xa_max"), 1)

            def xa_head(h, more):
                dve.wait_ge(sem("xa_v_turned"), h + 1)
                V.tensor_copy(CVT[:], PS[0][:].rearrange("p (c f) -> p c f", c=2)).then_inc(sem("xa_v_tokens"), 1)
                dve.wait_ge(sem("xa_exp"), h * SC + SC)
                chain.link(V.reciprocal(CSR[:], CSU[:]))
                TT(CP[:], CP[:], CSR[:].unsqueeze(2).broadcast_to([P, SC, MEM]), ALU.mult).then_inc(sem("xa_scaled"), 1)
                if more:
                    xa_stage(h + 1)
                    xa_maxima(h + 1)
                for e in range(2):
                    dve.wait_ge(sem("xa_pv"), h * 2 + e + 1)
                    free_product(PROD0["xa"] + e, h * 2)
                    V.tensor_copy(PR[:, (PROD0["xa"] + e) % 2, :], PS[(5, 0)[e]][:]).then_inc(s_pr, 1)
                for e in range(2):
                    low(PROD0["xa"] + e, h * 2, row(XOH, h * 2 + e), row(XOL, h * 2 + e))
            xa_stage(0)
            xa_maxima(0)
            with dve.Fori(0, XA_HEADS - 1) as h:
                chain.enter(h, 2)
                xa_head(h, True)
                chain.leave(XA_HEADS - 1)
            xa_head(XA_HEADS - 1, False)
            branch("xa_o")
            boundary(3, "post_xa", "g_xa_post", 1.0)
            norm("ffn2", "norm_ffn2", "g_ffn2_pre")
            ffn(2)
            boundary(4, "post_ffn2", "g_ffn2_post", 0.5)

        @block.tensor
        def _(pe):
            MM, TR = nc.tensor.matmul, nc.tensor.transpose

            def gemm(name, s, i, g, hi, lo, k0=0, n=S, made=None, half=None):
                c, nb, per = SLOT0[name] + s, WIDTH[SLOT0[name] + s], PER_TILE.get(name, 1)
                first, last = s % per == 0, s % per == per - 1
                tile = TILE0[name] + s // per
                pe.wait_ge(s_lo, i * g + c + 1)
                if first and tile >= 2 and half != 1:
                    pe.wait_ge(s_acc, i * (g // per) + tile - 1)
                parts = ((WH, hi), (WH, lo), (WL, hi))
                for k in range(nb) if half is None else range(half * nb // 2, (half + 1) * nb // 2):
                    if made is not None and s < 4:
                        pe.wait_ge(s_pl, made + k0 + k + 1)
                    for r, (w, a) in enumerate(parts):
                        ins = MM(ACC[tile % 2][:, 0:n], w[:, c % HL_RING, k * P:(k + 1) * P], a[:, k0 + k, 0:n],
                                 start=first and r == 0 and k == 0, stop=last and r == 2 and k == nb - 1)
                if half != 0:
                    ins.then_inc(s_used, 1)

            def stage(name, hi, lo, product, n=S):
                run_stage(pe, name, lambda s, i, g: gemm(name, s, i, g, hi, lo, 0, n, PROD0[product]))

            def total(name, n=S, ks=None):
                q0, count = SUM_SQ0[name], SUMS[SUM_N[name]][1]
                if SUM_N[name] and name != "ssd1":
                    pe.wait_ge(s_rstd, SUM_N[name])
                for k in range(count):
                    pe.wait_ge(s_sq, q0 + k + 1)
                    MM(sum_bank(name)[:, 0:n], ones, SQ[:, (q0 + k) % 2, 0:n], start=k == 0, stop=k == count - 1).then_inc(s_squsd, 1)

            def branch_total(b):
                pe.wait_ge(s_fsq, EV_RING + (b + 1) * DK)
                MM(PS[5][:], ones, SSQ[:], start=True, stop=True).then_inc(s_psum, 1)

            def done(name):
                return PROD0[name] + dict(PRODUCTS)[name]

            def narrow_rows(bank, w_hi, w_lo, cols):
                for k in range(DK):
                    for r, (w, a) in enumerate(((w_hi, HH), (w_hi, HL), (w_lo, HH))):
                        ins = MM(PS[bank][0:cols, :], w[:, k, :], a[:, k, :], start=r == 0 and k == 0,
                                 stop=r == 2 and k == DK - 1)
                return ins

            def token_major(bank, cols):
                for c in range(SC):
                    ins = TR(PS[bank][:, c * cols:(c + 1) * cols], NROWS[0:cols, c * P:(c + 1) * P],
                             ident[0:cols, 0:cols])
                return ins

            def turn(bank, src, blocks, to=0):
                for c in range(blocks):
                    ins = TR(PS[bank][:, to + c * P:to + (c + 1) * P], src[:, c * P:(c + 1) * P], ident)
                return ins

            pe.wait_ge(s_in, 64)
            total("pre")


            def half_turn(t):
                pe.wait_ge(s_acc, TILE0["nsa_rope"] + t + 1)
                if t >= 2:
                    pe.wait_ge(sem("nsa_roped"), t - 1)
                MM(PS[t % 2][:], const("nsa_rot"), EV[:, (EV0["nsa_rope"] + t) % EV_RING, :], start=True,
                   stop=True).then_inc(sem("nsa_turned_half"), 1)
            for s in range(COUNT["nsa_rope"]):
                gemm("nsa_rope", s, 0, 4, HH, HL, made=PROD0["norm_pre"])
                if s:
                    half_turn(s - 1)
            gemm("nsa_plain", 0, 0, 4, HH, HL)
            half_turn(COUNT["nsa_rope"] - 1)
            for s in range(1, COUNT["nsa_plain"]):
                gemm("nsa_plain", s, 0, 4, HH, HL)
            pe.wait_ge(sem("gate_w_lo"), 1)
            narrow_rows(2, WGH, WGL, 24).then_inc(sem("gate_rows"), 1)
            for n in range(2):
                pe.wait_ge(s_acc, TILE0["nsa_plain"] + n + 2)
                turn(3 + n, VN[:, 1 + n, :], SC).then_inc(sem("nsa_v_turned"), 1)
            pe.wait_ge(sem("gate_rows_copied"), 1)
            token_major(2, 24).then_inc(sem("gate_psum"), 1)

            pe.wait_ge(s_late["cmp_w"], 64)
            pe.wait_ge(sem("nsa_roped"), COUNT["nsa_rope"])
            for n, t in enumerate(("k", "v")):
                pe.wait_ge(sem("cmp_blocks"), n + 1)
                for j in range(2):
                    for b in range(16):
                        ins = MM(PS[n][:, j * 2 * N_CMP:(j + 1) * 2 * N_CMP], W1[t][:, b, j * P:(j + 1) * P],
                                 BLK[t][:, b, :], start=b == 0, stop=b == 15)
                ins.then_inc(sem("cmp_hidden"), 1)
            pe.wait_ge(sem("gate_sum"), 1)
            pe.wait_ge(sem("cmp_gelu"), 2)
            for g in range(2):
                for j in range(2):
                    MM(PS[2][DH * g:DH * (g + 1), 0:N_CMP], W2["k"][:, j, :], HG["k"][:, j, g * N_CMP:(g + 1) * N_CMP],
                       start=j == 0, stop=j == 1)
            for g in range(2):
                for j in range(2):
                    ins = MM(PS[2][0:N_CMP, P + DH * g:P + DH * (g + 1)], HG["v"][:, j, g * N_CMP:(g + 1) * N_CMP],
                             W2["v"][:, j, :], start=j == 0, stop=j == 1)
            ins.then_inc(sem("cmp_done"), 1)

            pe.wait_ge(sem("nsa_v_tokens"), 2)
            pe.wait_ge(sem("cmp_kv"), 1)
            pe.wait_ge(sem("gate_ready"), 1)

            def wide_scores(u):
                i, hh = divmod(u, 2)
                kw, rows = (i + 1) * P, slice(DH * hh, DH * (hh + 1))
                for b in range(2):
                    MM(PS[b][:, 0:kw], QST[rows, i * P:(i + 1) * P], QK[rows, 5 + b, 0:kw], start=True, stop=False)
                    MM(PS[b][:, i * P:kw], ident, const("causal"), start=False, stop=True)

            def cmp_scores(u):
                i, hh = divmod(u, 2)
                rows = slice(DH * hh, DH * (hh + 1))
                MM(PS[2][:, 0:N_CMP], QST[rows, i * P:(i + 1) * P], KCT[rows, 0:N_CMP], start=True, stop=False)
                MM(PS[2][:, 0:N_CMP], ident, const("cmp_mask")[:, i * 32:i * 32 + N_CMP], start=False,
                   stop=True).then_inc(sem("nsa_scored"), 1)

            with pe.Fori(0, NSA_PAIRS) as p:
                pe.wait_ge(sem("nsa_staged"), p + 1)
                wide_scores(0)
                cmp_scores(0)
                for u in range(8):
                    i, hh = divmod(u, 2)
                    rows, cols = slice(DH * hh, DH * (hh + 1)), slice(i * P, (i + 1) * P)
                    pe.wait_ge(sem("nsa_scaled"), p * 8 + u + 1)
                    turn(3, PB[:, 0:S], i + 1)
                    turn(4, PB[:, S:2 * S], i + 1)
                    TR(PS[2][0:N_CMP, P:2 * P], PB[:, 2 * S:2 * S + N_CMP], ident).then_inc(sem("nsa_turned"), 1)
                    if u < 7:
                        wide_scores(u + 1)
                    pe.wait_ge(sem("nsa_win_t"), p * 8 + u + 1)
                    if u < 7:
                        cmp_scores(u + 1)
                    pe.wait_ge(sem("nsa_sel_t"), p * 8 + u + 1)
                    for c in range(i + 1):
                        MM(PS[5][rows, cols], VS[:, c, rows], PTS[:, c, :], start=c == 0, stop=False)
                    for c in range(i + 1):
                        MM(PS[5][rows, cols], VW[:, c, rows], PTW[:, c, :], start=False, stop=False)
                    MM(PS[5][rows, cols], VCT[0:N_CMP, hh, :], PTC[0:N_CMP, :], start=False, stop=True).then_inc(
                        sem("nsa_pv"), 1)
                    gemm("ret_in", u // 2, p, 4, HH, HL, half=u % 2)

            def ret_head(i, q):
                h = i * 2 + q
                pe.wait_ge(sem("ret_v_staged"), h + 1)
                pe.wait_ge(sem("ret_staged"), h + 1)
                for e in range(2):
                    turn(e, EV[:, e, :], SC).then_inc(sem("ret_v_turned"), 1)
                for j in range(SC):
                    if j >= 2:
                        pe.wait_ge(sem("ret_decayed"), h * SC + j - 1)
                    MM(PS[(2, 5)[j % 2]][:, 0:S - j * P], RKS[:, j * P:(j + 1) * P], RQS[:, j * P:S], start=True,
                       stop=True).then_inc(sem("ret_scored"), 1)
                pe.wait_ge(sem("ret_v_tokens"), h * 2 + 2)
                for j in range(SC):
                    pe.wait_ge(sem("ret_decayed"), h * SC + j + 1)
                    for e in range(2):
                        ins = MM(PS[3 + e][:, j * P:S], RVT[:, j, e * P:(e + 1) * P], RSM[:, j, 0:S - j * P],
                                 start=j == 0, stop=j == SC - 1)
                ins.then_inc(sem("ret_pv"), 1)
                pe.wait_ge(sem("ret_raw"), h * 2 + 2)
                for e in range(2):
                    ins = MM(PS[0][:], ones_ret, row(ORT, h * 2 + e), start=e == 0, stop=e == 1)
                ins.then_inc(sem("ret_mean"), 1)
                gemm("z_ret", 2 * q, i, 4, HH, HL)
                pe.wait_ge(sem("ret_sq"), h * 2 + 2)
                for e in range(2):
                    ins = MM(PS[1][:], ones_ret, EV[:, 2 + e, :], start=e == 0, stop=e == 1)
                ins.then_inc(sem("ret_var"), 1)
                gemm("z_ret", 2 * q + 1, i, 4, HH, HL)
            with pe.Fori(0, RET_HEADS // 2) as i:
                for q in range(2):
                    ret_head(i, q)
            stage("z_nsa", HH, HL, "norm_pre")

            def merge_slot(s, i, g):
                hi, lo = ((HH, HL), (GAH, GAL), (HH, HL), (GRH, GRL))[s % 4]
                if s in (1, 3):
                    pe.wait_ge(s_pl, done("gates"))
                gemm("merge", s, i, g, hi, lo)
            run_stage(pe, "merge", merge_slot)
            stage("out1", MGH, MGL, "merge")
            branch_total(0)
            total("ffn1")

            def ffn(n):
                stage(f"ffn{n}_up", HH, HL, f"norm_ffn{n}")
                run_stage(pe, f"ffn{n}_down", lambda s, i, g: gemm(f"ffn{n}_down", s, i, g, AH, AL, (s % 2) * HALF_FK,
                                                                   made=PROD0[f"ffn{n}"]))
            ffn(1)
            branch_total(1)
            total("mix")

            stage("sb_qkv", HH, HL, "norm_mix")
            tri, neg = const("neg_incl"), const("neg_ones")

            def place_of(hh, j):
                return ((hh, 0), (2 + hh, 0), (4, 2 * P * hh), (2 + hh, 3 * P))[j]

            def sb_pair(i, q):
                p = i * 2 + q

                def scores(hh, j):
                    b, at = place_of(hh, j)
                    rows = slice(DH * hh, DH * (hh + 1))
                    return MM(PS[b][:, at:at + S - j * P], BKS[rows, j * P:(j + 1) * P], BQS[rows, j * P:S],
                              start=at == 0, stop=True, skip_group_check=True)
                pe.wait_ge(sem("sb_staged"), p + 1)
                scores(0, 2).then_inc(sem("sb_first_half"), 1)
                for b in range(4):
                    ins = scores(b % 2, b // 2)
                    if b >= 2:
                        ins = scores(b % 2, 3)
                    ins.then_inc(sem("sb_scored"), 1)
                pe.wait_ge(sem("sb_first_half"), p + 1)
                scores(1, 2).then_inc(sem("sb_scored"), 1)
                pe.wait_ge(sem("sb_out"), p + 1)
                turn(5, BVS, SC).then_inc(sem("sb_v_turned"), 1)
                for s in range(2):
                    gemm("ssd_early", 2 * q + s, i, 4, HH, HL)
                pe.wait_ge(sem("sb_softplus_masked"), p * 5 + 5)
                for b in range(5):
                    for hh, j in ([(0, 0)], [(1, 0)], [(0, 1), (0, 3)], [(1, 1), (1, 3)], [(0, 2), (1, 2)])[b]:
                        at, end = place_of(hh, j)[1], place_of(hh, j)[1] + S - j * P
                        for later in range(j, SC):
                            sb_, sat = place_of(hh, later)
                            n = S - later * P
                            ins = MM(PS[b][:, end - n:end], tri if later == j else neg, SPB[:, sb_, sat:sat + n],
                                     start=False, stop=True, skip_group_check=True)
                    ins.then_inc(sem("sb_suffixed"), 1)
                pe.wait_ge(sem("sb_v_tokens"), p + 1)
                for b in range(5):
                    pe.wait_ge(sem("sb_exp_masked"), p * 5 + b + 1)
                    for hh, j in ([(0, 0)], [(1, 0)], [(0, 1), (0, 3)], [(1, 1), (1, 3)], [(0, 2), (1, 2)])[b]:
                        at, rows = place_of(hh, j)[1], slice(DH * hh, DH * (hh + 1))
                        ins = MM(PS[5][rows, j * P:S], BVT[:, j, rows], sb_tmp(b)[:, at:at + S - j * P], start=j == 0,
                                 stop=j == 2, skip_group_check=True)
                ins.then_inc(sem("sb_pv"), 1)
            with pe.Fori(0, SB_PAIRS // 2) as i:
                for q in range(2):
                    sb_pair(i, q)
            total("attn")

            stage("ssd_late", HH, HL, "norm_mix")
            pe.wait_ge(sem("dt_w_lo"), 1)
            narrow_rows(0, WDH, WDL, SSD_HEADS).then_inc(sem("dt_rows"), 1)
            pe.wait_ge(sem("conv_silu"), 4)
            for g in range(2):
                turn(3 + g, XB[:, 2 * g, :], SC).then_inc(sem("ssd_bt"), 1)
            pe.wait_ge(sem("dt_rows_copied"), 1)
            token_major(0, SSD_HEADS).then_inc(sem("dt_psum"), 1)
            pe.wait_ge(sem("adt"), 1)
            MM(PS[1][:, 0:64], const("later"), ADT[:].rearrange("p c h -> p (c h)"), start=True, stop=True)
            MM(PS[2][:, 0:64], ones, ADT[:].rearrange("p c h -> p (c h)"), start=True, stop=True).then_inc(sem("dt_sums"), 1)
            for g in range(2):
                for c in range(SC):
                    cols = slice(c * P, (c + 1) * P)
                    ins = MM(PS[(5, 0)[g]][:, cols], XB[:, 2 * g, cols], XB[:, 2 * g + 1, cols], start=True, stop=True)
                ins.then_inc(sem("ssd_cb_psum"), 1)
            pe.wait_ge(sem("ssd_b_tokens"), 2)
            pe.wait_ge(sem("dt_decays"), 1)
            for g in range(2):
                with pe.Fori(0, 4) as p:
                    n = p + 4 * g
                    pe.wait_ge(sem("ssd_lhs"), n + 1)
                    for hh in range(2):
                        for c in range(SC):
                            ins = MM(PS[1 + hh][:, c * P:(c + 1) * P], LSG[:, c, hh, :], const("upper_incl"), start=True,
                                     stop=True)
                    ins.then_inc(sem("ssd_seg"), 1)
                    for c in range(1, SC):
                        ins = MM(PS[3][:, c * P:(c + 1) * P], ARP[:, c, :], const("upper_incl"), start=True, stop=True)
                    ins.then_inc(sem("ssd_rows"), 1)
                    pe.wait_ge(sem("ssd_staged"), n + 1)
                    turn(0, XST, SC).then_inc(sem("ssd_x_turned"), 1)
                    pe.wait_ge(sem("ssd_x12"), n + 1)
                    for c in range(SC - 1):
                        ins = MM(PS[4][:, c * P:(c + 1) * P], BTK[:, g, c, :], X2[:, c].rearrange("p h d -> p (h d)"),
                                 start=True, stop=True)
                    ins.then_inc(sem("ssd_new"), 1)
                    pe.wait_ge(sem("ssd_m"), n * 2 + 2)
                    for hh in range(2):
                        for c in range(SC):
                            MM(PS[5][DH * hh:DH * (hh + 1), c * P:(c + 1) * P], X1[:, c, hh, :], LM[:, hh, c, :],
                               start=True, stop=True)
                    pe.wait_ge(sem("ssd_states"), n + 1)
                    for c in range(1, SC):
                        ins = MM(PS[0][:, c * P:(c + 1) * P], STT_[:, c - 1, :], XB[:, 2 * g + 1, c * P:(c + 1) * P],
                                 start=True, stop=True)
                    ins.then_inc(sem("ssd_y"), 1)
                    pe.wait_ge(sem("ssd_row_exp"), n + 1)
            total("ssd0")
            total("ssd1")
            run_stage(pe, "out2", lambda s, i, g: gemm("out2", s, i, g, *((OSH, OSL), (YSH, YSL))[s % 2],
                                                       made=PROD0[("norm_attn", "norm_ssd")[s % 2]]))
            branch_total(2)
            total("xa")

            stage("xa_q", HH, HL, "norm_xa")
            total("mem", MEM)
            stage("xa_kv", MH, ML, "norm_mem", MEM)

            def xa_scores(h):
                pe.wait_ge(sem("xa_staged"), h + 1)
                for i in range(SC):
                    for e in range(2):
                        ins = MM(PS[1 + i // 2][:, (i % 2) * MEM:(i % 2 + 1) * MEM], CQS[:, e, i * P:(i + 1) * P],
                                 CKS[:, e, :], start=e == 0, stop=e == 1)
                ins.then_inc(sem("xa_scored"), 1)

            def xa_head(h, more):
                pe.wait_ge(s_pr, h * 2 + PROD0["xa"])
                for mc in range(2):
                    for e in range(2):
                        ins = TR(PS[0][:, (mc * 2 + e) * P:(mc * 2 + e + 1) * P], CVS[:, e, mc * P:(mc + 1) * P], ident)
                ins.then_inc(sem("xa_v_turned"), 1)
                pe.wait_ge(sem("xa_scaled"), h + 1)
                for mc in range(2):
                    for i in range(SC):
                        ins = TR(PS[3 + mc][:, i * P:(i + 1) * P], CP[:, i, mc * P:(mc + 1) * P], ident)
                    ins.then_inc(sem("xa_turned"), 1)
                if more:
                    xa_scores(h + 1)
                pe.wait_ge(sem("xa_v_tokens"), h + 1)
                pe.wait_ge(sem("xa_probs_t"), h * 2 + 2)
                for e in range(2):
                    for mc in range(2):
                        ins = MM(PS[(5, 0)[e]][:], CVT[:, mc, e * P:(e + 1) * P], CPT[:, mc, :], start=mc == 0,
                                 stop=mc == 1)
                    ins.then_inc(sem("xa_pv"), 1)
            xa_scores(0)
            with pe.Fori(0, XA_HEADS - 1) as h:
                xa_head(h, True)
            xa_head(XA_HEADS - 1, False)
            stage("xa_o", XOH, XOL, "xa")
            branch_total(3)
            total("ffn2")
            ffn(2)
            branch_total(4)


def shape_constants():
    k, m = np.arange(P)[:, None], np.arange(P)[None, :]
    rot = np.zeros((P, P))
    for d in range(P):
        if d % DH < 8:
            rot[d + 8, d] = 1
        elif d % DH < 16:
            rot[d - 8, d] = 1
    q = np.arange(S).reshape(SC, P).T[:, :, None]
    seen = (np.arange(32)[None, None, :] * CMP_STRIDE + CMP_LEN - 1 <= q)
    parts = {"ident": np.eye(P), "ones": np.ones((P, P)), "ones_ret": np.full((P, P), 1.0 / RET_DV), "nsa_rot": rot,
             "causal": np.where(m > k, NEG, 0.0), "neg_incl": -1.0 * (k >= m), "neg_ones": -np.ones((P, P)),
             "upper_incl": 1.0 * (k <= m), "later": 1.0 * (k > m),
             "cmp_mask": np.where(seen, 0.0, NEG).reshape(P, -1), "cmp_keep": (1.0 * seen).reshape(P, -1)}
    consts = np.concatenate([parts[n] for n, _ in CONSTS], axis=1).astype(np.float32)

    pos = np.arange(S, dtype=np.float32)
    rope = np.zeros((P, 4, S), np.float32)
    rope[:, 0] = 1.0
    inv = (1.0 / (500000.0 ** (np.arange(0, 16, 2, dtype=np.float32) / 16))).astype(np.float32)
    for d in range(P):
        if d % DH < 16:
            ang = pos * inv[d % 8]
            rope[d, 0] = np.cos(ang)
            rope[d, 1] = np.sin(ang) * (-1 if d % DH < 8 else 1)
    inv = (1.0 / (10000.0 ** np.linspace(0.0, 1.0, RET_DK // 2, dtype=np.float32))).astype(np.float32)
    ang = pos[None, :] * inv[np.arange(P) % 64][:, None]
    rope[:, 2] = np.cos(ang)
    rope[:, 3] = np.sin(ang) * np.where(np.arange(P) < 64, 1, -1)[:, None]

    dist = np.arange(S)[None, :] - np.arange(P)[:, None]
    log_g = np.log(1.0 - 2.0 ** (-5.0 - np.arange(RET_HEADS)))
    decay = np.where(dist[:, None, :] >= 0, np.exp(np.maximum(dist, 0)[:, None, :] * log_g[None, :, None]), 0.0)
    decay = (decay * RET_DK ** -0.5).astype(np.float32)
    return consts, rope, decay


def tiles(w):
    kk, mm = w.shape
    return w.reshape(kk // P, P, mm // P, P).transpose(1, 2, 0, 3)


def flat(w):
    return w.reshape(P, -1)


def columns(v):
    return v.reshape(-1, P).T


def stream(w_in, w_nsa_o, w_ret_o, w_out, ffn, w_in2, w_out2, wq, wkv, wo, pairs):
    at = np.cumsum([0, 512, 128, 128, 128, 128, 128, 128, 24, 512, 512, 512, 1024, 1024, D, D])
    (q_n, k_c, v_c, k_s, v_s, k_w, v_w, _, z_n, q_r, k_r, v_r, z_r, m_a, m_b) = [
        w_in[:, a:b] for a, b in zip(at[:-1], at[1:])]
    out = [flat(tiles(w)) for w in (q_n[:, pairs], k_c, k_s, k_w, v_c, v_s, v_w)]
    by_pair = [t.reshape(P, NSA_PAIRS, 2, DK, P) for t in (np.concatenate([tiles(q_r), tiles(k_r)], axis=1), tiles(v_r))]
    out += [flat(np.concatenate(by_pair, axis=2)), flat(tiles(z_r)), flat(tiles(z_n[:, pairs]))]
    ma, mb, ya, yb = tiles(m_a), tiles(m_b), tiles(w_nsa_o[pairs]), tiles(w_ret_o)
    for m in range(DK):
        out += [flat(ma[:, m]), flat(ya[:, m]), flat(mb[:, m]), flat(yb[:, m])]
    out.append(flat(tiles(w_out)))

    def feed_forward(gu, down):
        g, u = tiles(gu[:, :FF]), tiles(gu[:, FF:])
        return [flat(np.stack([g, u], axis=2)), flat(tiles(down))]
    out += feed_forward(*ffn[0])
    q, k, v, z, xbc, _ = np.split(w_in2, [1024, 2048, 3072, 4096, 4096 + CONV_TILES * P], axis=1)
    out += [flat(tiles(w)) for w in (q, k, v)]
    tx, tz = tiles(xbc)[:, CONV_ORDER], tiles(z)
    out += [flat(np.stack([tx[:, :8], tz], axis=2)), flat(tx[:, 8:])]
    out += [flat(tiles(w)) for w in (w_out2, wq, wkv, wo)]
    out += feed_forward(*ffn[1])
    return np.concatenate(out, axis=1)


def narrow(w):
    return w.reshape(DK, P, -1).transpose(1, 0, 2)


def kernel(x, norm_pre, w_in, b_nsa_gate, cmp_pe_k, cmp_w1_k, cmp_w2_k, cmp_pe_v, cmp_w1_v, cmp_w2_v, w_nsa_o,
           w_ret_o, w_out, norm_post, mem_2, ffn1_pre_g_2, ffn1_w_gu_2, ffn1_w_down_2, ffn1_post_g_2, mix_pre_g_2,
           w_in_2, conv_w_2, conv_b_2, dt_bias_2, a_log_2, d_skip_2, ssd_norm_g_2, attn_norm_g_2, w_out_2,
           mix_post_g_2, xa_pre_g_2, mem_g_2, xa_wq_2, xa_wkv_2, xa_wo_2, xa_post_g_2, ffn2_pre_g_2, ffn2_w_gu_2,
           ffn2_w_down_2, ffn2_post_g_2):
    import concourse.bacc as bacc
    from concourse.bass_utils import run_bass_kernel_spmd

    a = {n: np.asarray(v) for n, v in locals().items() if hasattr(v, "shape")}

    pairs = np.concatenate([np.arange(DH) + DH * h for p in range(NSA_PAIRS) for h in (p, p + NSA_PAIRS)])

    def spread(v):
        return np.broadcast_to(v.reshape(1, -1), (P, v.size))

    def positions(pe):
        v = pe.reshape(16, 2, DH).transpose(2, 1, 0).reshape(DH, 32)
        return np.concatenate([v, v], axis=0)

    def hidden(w1):
        return w1.reshape(16, 2, DH, CMP_HIDDEN).transpose(1, 2, 0, 3).reshape(P, 16, CMP_HIDDEN)

    conv_w = a["conv_w_2"][0]
    values = {
        "g_pre": columns(a["norm_pre"]), "g_post": columns(a["norm_post"]),
        "g_ffn1_pre": columns(a["ffn1_pre_g_2"][0]), "g_ffn1_post": columns(a["ffn1_post_g_2"][0]),
        "g_mix_pre": columns(a["mix_pre_g_2"][0]), "g_attn": columns(a["attn_norm_g_2"][0]),
        "g_ssd": columns(a["ssd_norm_g_2"][0]), "g_mix_post": columns(a["mix_post_g_2"][0]),
        "g_xa_pre": columns(a["xa_pre_g_2"][0]), "g_mem": columns(a["mem_g_2"][0]),
        "g_xa_post": columns(a["xa_post_g_2"][0]), "g_ffn2_pre": columns(a["ffn2_pre_g_2"][0]),
        "g_ffn2_post": columns(a["ffn2_post_g_2"][0]), "conv_b": columns(a["conv_b_2"][0])[:, CONV_ORDER],
        "conv_w": np.concatenate([columns(conv_w[k])[:, CONV_ORDER] for k in range(CONV_K)], axis=1),
        "d_skip": columns(np.repeat(a["d_skip_2"][0], SSD_P)), "gate_b": spread(a["b_nsa_gate"]),
        "dt_b": spread(a["dt_bias_2"][0]), "a_log": spread(a["a_log_2"][0]),
        "pe_k": positions(a["cmp_pe_k"]), "pe_v": positions(a["cmp_pe_v"]),
    }
    consts, rope, decay = shape_constants()
    w2in = a["w_in_2"][0]
    data = {
        "xT": a["x"][0].T.reshape(DK, P, S).transpose(1, 0, 2),
        "mem_t": a["mem_2"][0].T.reshape(DK, P, MEM).transpose(1, 0, 2),
        "w_all": stream(a["w_in"], a["w_nsa_o"], a["w_ret_o"], a["w_out"],
                        [(a["ffn1_w_gu_2"][0], a["ffn1_w_down_2"][0]), (a["ffn2_w_gu_2"][0], a["ffn2_w_down_2"][0])],
                        w2in, a["w_out_2"][0], a["xa_wq_2"][0], a["xa_wkv_2"][0], a["xa_wo_2"][0], pairs),
        "params": np.concatenate([values[n] for n, _ in PARAMS], axis=1),
        "consts": consts, "rope": rope, "decay": decay,
        "w_gate": narrow(a["w_in"][:, 1280:1304]), "w_dt": narrow(w2in[:, -SSD_HEADS:]),
        "w1k": hidden(a["cmp_w1_k"]), "w1v": hidden(a["cmp_w1_v"]),
        "w2k": a["cmp_w2_k"].reshape(2, P, DH).transpose(1, 0, 2),
        "w2v": a["cmp_w2_v"].reshape(2, P, DH).transpose(1, 0, 2),
    }
    nc = bacc.Bacc("TRN2", target_bir_lowering=False, num_devices=1)
    arrays, args = {}, []
    for name, v in data.items():
        v = np.ascontiguousarray(v)
        arrays[name] = v
        args.append(nc.dram_tensor(name, v.shape, mybir.dt.from_np(v.dtype), kind="ExternalInput").ap())
    args.append(nc.dram_tensor("out_t", (P, DK, S), F32, kind="ExternalOutput").ap())
    block_program(nc, *args)
    r = run_bass_kernel_spmd(nc, [arrays], core_ids=[0])
    out = np.asarray(r.results[0]["out_t"])
    return np.ascontiguousarray(out.transpose(1, 0, 2).reshape(D, S).T).reshape(a["x"].shape)
```
